# Optimizing a Trainium2 kernel written in Bass

```python
import math
import jax
import jax.numpy as jnp
from jax import lax
import numpy as np

D_MODEL = 2048
BATCH = 1
SEQ = 256
DEPTH = 2

CHUNK = 64
Q_BLOCK = 128
N_MEM = 256
MAX_OFFSET = 4096
H_A = 4
DK_A = 64
DV_A = 2 * DK_A
H_B = 6
D_B = 128
FORGET_BIAS_CENTRE = 2.0
H_C = 6
Q_LORA = 512
KV_LORA = 256
D_NOPE = 64
D_ROPE = 32
DV_C = 128
ROPE_THETA = 10000.0
D_MIX = H_A * DV_A + H_B * D_B + H_C * DV_C
SPLIT_SIZES = (H_A * 2 * DK_A, H_A * 2 * DK_A, H_A * DV_A,
               H_B * D_B, H_B * D_B, H_B * D_B, H_B,
               Q_LORA, KV_LORA, D_ROPE)
D_IN = 2 * H_A * 2 * DK_A + H_A * DV_A + 3 * H_B * D_B + H_B + Q_LORA + KV_LORA + D_ROPE
N_BUCKETS = 32
MAX_DISTANCE = 512
H_X = 4
D_X = 128
D_FF = 4096
CONV_W = 3
EPS = 1e-6
NEG_INF = -1e30

kernel_name = "hymba_style_diff_fox_mla_streaming_trunk"

def _split_points():
    pts, acc = [], 0
    for s in SPLIT_SIZES[:-1]:
        acc += s
        pts.append(acc)
    return pts

def rms(x):
    xf = x.astype(jnp.float32)
    return (xf * lax.rsqrt(jnp.mean(xf * xf, axis=-1, keepdims=True) + EPS)).astype(x.dtype)

def rmsnorm(x, g):
    return rms(x) * g.astype(x.dtype)

def rope_angles(positions, dtype):
    inv = ROPE_THETA ** (-jnp.arange(0, D_ROPE, 2, dtype=jnp.float32) / D_ROPE)
    ang = positions.astype(jnp.float32)[..., None] * inv
    return jnp.cos(ang).astype(dtype), jnp.sin(ang).astype(dtype)

def apply_rope(t, cos, sin):
    t1, t2 = t[..., :D_ROPE // 2], t[..., D_ROPE // 2:]
    return jnp.concatenate([t1 * cos - t2 * sin, t2 * cos + t1 * sin], axis=-1)

def t5_bucket(rel):
    half = N_BUCKETS // 2
    max_exact = half // 2
    ret = jnp.where(rel > 0, half, 0)
    n = jnp.abs(rel)
    nf = jnp.maximum(n, 1).astype(jnp.float32)
    large = max_exact + (jnp.log(nf / max_exact) / math.log(MAX_DISTANCE / max_exact)
                         * (half - max_exact)).astype(jnp.int32)
    large = jnp.minimum(large, half - 1)
    return ret + jnp.where(n < max_exact, n, large)

def to_blocks(t):
    b, s = t.shape[0], t.shape[1]
    t = t.reshape((b, s // Q_BLOCK, Q_BLOCK) + t.shape[2:])
    return jnp.moveaxis(t, 1, 0)

def from_blocks(t):
    t = jnp.moveaxis(t, 0, 1)
    return t.reshape((t.shape[0], t.shape[1] * t.shape[2]) + t.shape[3:])

def hybrid_mixer(h, positions, rel_bias, w_in, b_forget, lam, lam_init,
                 q_norm, kv_norm, w_uq, w_ukv, head_norm, w_out):
    B, S, _ = h.shape
    f32 = jnp.float32
    qa, ka, va, qb, kb, vb, fb, cq, ckv, kr = jnp.split(h @ w_in, _split_points(), axis=-1)
    qa = qa.reshape(B, S, H_A, 2, DK_A)
    ka = ka.reshape(B, S, H_A, 2, DK_A)
    va = va.reshape(B, S, H_A, DV_A)
    lam = lam.astype(f32)
    lam_val = jnp.exp(jnp.sum(lam[0] * lam[1])) - jnp.exp(jnp.sum(lam[2] * lam[3])) + lam_init
    qb = qb.reshape(B, S, H_B, D_B)
    kb = kb.reshape(B, S, H_B, D_B)
    vb = vb.reshape(B, S, H_B, D_B)
    log_f = jax.nn.log_sigmoid(fb.astype(f32) + b_forget.astype(f32))
    cum_f = jnp.cumsum(log_f, axis=1)
    cum_f_k = jnp.transpose(cum_f, (0, 2, 1))
    cq = rmsnorm(cq, q_norm)
    ckv = rmsnorm(ckv, kv_norm)
    qc = (cq @ w_uq).reshape(B, S, H_C, D_NOPE + D_ROPE)
    kvc = (ckv @ w_ukv).reshape(B, S, H_C, D_NOPE + DV_C)
    qn, qr = qc[..., :D_NOPE], qc[..., D_NOPE:]
    kn, vc = kvc[..., :D_NOPE], kvc[..., D_NOPE:]
    cos, sin = rope_angles(positions, h.dtype)
    qr = apply_rope(qr, cos[:, :, None], sin[:, :, None])
    kr = apply_rope(kr, cos, sin)
    k_idx = jnp.arange(S)

    def attend_block(args):
        blk, qa_b, qb_b, fq_b, qn_b, qr_b, pq_b = args
        q_idx = blk * Q_BLOCK + jnp.arange(Q_BLOCK)
        chunk_ok = (k_idx[None, :] // CHUNK) <= (q_idx[:, None] // CHUNK)
        frame_ok = k_idx[None, :] <= q_idx[:, None]
        bucket = t5_bucket(positions[:, None, :] - pq_b[:, :, None])
        bias = jnp.moveaxis(rel_bias[bucket], -1, 1)[:, :, None].astype(f32)
        s_a = jnp.einsum('bqhmd,bkhmd->bhmqk', qa_b, ka).astype(f32) * DK_A ** -0.5 + bias
        p_a = jax.nn.softmax(jnp.where(chunk_ok, s_a, NEG_INF), axis=-1)
        p_a = p_a[:, :, 0] - lam_val * p_a[:, :, 1]
        o_a = jnp.einsum('bhqk,bkhd->bqhd', p_a.astype(va.dtype), va)
        s_b = (jnp.einsum('bqhd,bkhd->bhqk', qb_b, kb).astype(f32) * D_B ** -0.5
               + jnp.transpose(fq_b, (0, 2, 1))[..., None] - cum_f_k[:, :, None, :])
        p_b = jax.nn.softmax(jnp.where(frame_ok, s_b, NEG_INF), axis=-1)
        o_b = jnp.einsum('bhqk,bkhd->bqhd', p_b.astype(vb.dtype), vb)
        s_c = (jnp.einsum('bqhd,bkhd->bhqk', qn_b, kn)
               + jnp.einsum('bqhr,bkr->bhqk', qr_b, kr)).astype(f32) * (D_NOPE + D_ROPE) ** -0.5
        p_c = jax.nn.softmax(jnp.where(chunk_ok, s_c, NEG_INF), axis=-1)
        o_c = jnp.einsum('bhqk,bkhd->bqhd', p_c.astype(vc.dtype), vc)
        return o_a, o_b, o_c

    n_blk = S // Q_BLOCK
    o_a, o_b, o_c = lax.map(attend_block, (jnp.arange(n_blk), to_blocks(qa), to_blocks(qb),
                                           to_blocks(cum_f), to_blocks(qn), to_blocks(qr),
                                           to_blocks(positions)))
    o_a = rms(from_blocks(o_a)) * (1.0 - lam_init)
    o_b = rms(from_blocks(o_b))
    o_c = rms(from_blocks(o_c))
    o = jnp.concatenate([o_a.reshape(B, S, -1), o_b.reshape(B, S, -1), o_c.reshape(B, S, -1)],
                        axis=-1) * head_norm.astype(h.dtype)
    return o @ w_out

def memory_xattn(h, mem_n, wq, wkv, wo):
    B, S, _ = h.shape
    q = (h @ wq).reshape(B, S, H_X, D_X)
    k, v = jnp.split(mem_n @ wkv, 2, axis=-1)
    k = k.reshape(B, N_MEM, H_X, D_X)
    v = v.reshape(B, N_MEM, H_X, D_X)
    s = jnp.einsum('bqhd,bkhd->bhqk', q, k).astype(jnp.float32) * D_X ** -0.5
    p = jax.nn.softmax(s, axis=-1)
    o = jnp.einsum('bhqk,bkhd->bqhd', p.astype(v.dtype), v).reshape(B, S, H_X * D_X)
    return o @ wo

def conv_ffn(h, w_up, conv_w, conv_b, w_down):
    S = h.shape[1]
    u = h @ w_up
    up = jnp.pad(u, ((0, 0), (CONV_W - 1, 0), (0, 0)))
    c = conv_b.astype(h.dtype)
    for tap in range(CONV_W):
        c = c + up[:, tap:tap + S] * conv_w[tap]
    gate, val = jnp.split(c, 2, axis=-1)
    return (jax.nn.gelu(gate, approximate=True) * val) @ w_down

def setup_inputs(seed: int = 0) -> dict:
    key = jax.random.key(seed)
    ks = jax.random.split(key, 22)
    f32 = jnp.float32

    def nrm(k, shape, scale):
        return jax.random.normal(k, shape, f32) * scale

    def gain(k, shape):
        return 1.0 + 0.05 * jax.random.normal(k, shape, f32)

    x = nrm(ks[0], (BATCH, SEQ, D_MODEL), 1.0)
    mem = nrm(ks[1], (BATCH, N_MEM, D_MODEL), 1.0)
    offset = jax.random.randint(ks[2], (BATCH, 1), 0, MAX_OFFSET, dtype=jnp.int32)
    positions = offset + jnp.arange(SEQ, dtype=jnp.int32)[None, :]
    rel_bias = nrm(ks[3], (N_BUCKETS, H_A), 0.5)
    w_in = nrm(ks[4], (DEPTH, D_MODEL, D_IN), D_MODEL ** -0.5)
    b_forget = FORGET_BIAS_CENTRE + 0.5 * jax.random.normal(ks[5], (DEPTH, H_B), f32)
    lam = nrm(ks[6], (DEPTH, 4, DK_A), 0.1)
    q_norm = gain(ks[7], (DEPTH, Q_LORA))
    kv_norm = gain(ks[8], (DEPTH, KV_LORA))
    w_uq = nrm(ks[9], (DEPTH, Q_LORA, H_C * (D_NOPE + D_ROPE)), Q_LORA ** -0.5)
    w_ukv = nrm(ks[10], (DEPTH, KV_LORA, H_C * (D_NOPE + DV_C)), KV_LORA ** -0.5)
    head_norm = gain(ks[11], (DEPTH, D_MIX))
    w_out = nrm(ks[12], (DEPTH, D_MIX, D_MODEL), D_MIX ** -0.5)
    norm_gains = gain(ks[13], (DEPTH, 6, D_MODEL))
    mem_norm = gain(ks[14], (DEPTH, D_MODEL))
    wq_x = nrm(ks[15], (DEPTH, D_MODEL, H_X * D_X), D_MODEL ** -0.5)
    wkv_x = nrm(ks[16], (DEPTH, D_MODEL, 2 * H_X * D_X), D_MODEL ** -0.5)
    wo_x = nrm(ks[17], (DEPTH, H_X * D_X, D_MODEL), (H_X * D_X) ** -0.5)
    w_up = nrm(ks[18], (DEPTH, D_MODEL, 2 * D_FF), D_MODEL ** -0.5)
    conv_w = nrm(ks[19], (DEPTH, CONV_W, 2 * D_FF), CONV_W ** -0.5)
    conv_b = nrm(ks[20], (DEPTH, 2 * D_FF), 0.02)
    w_down = nrm(ks[21], (DEPTH, D_FF, D_MODEL), D_FF ** -0.5)
    return {"x": x, "mem": mem, "positions": positions, "rel_bias": rel_bias,
            "w_in": w_in, "b_forget": b_forget, "lam": lam, "q_norm": q_norm,
            "kv_norm": kv_norm, "w_uq": w_uq, "w_ukv": w_ukv, "head_norm": head_norm,
            "w_out": w_out, "norm_gains": norm_gains, "mem_norm": mem_norm,
            "wq_x": wq_x, "wkv_x": wkv_x, "wo_x": wo_x, "w_up": w_up,
            "conv_w": conv_w, "conv_b": conv_b, "w_down": w_down}

def reference(x, mem, positions, rel_bias, w_in, b_forget, lam, q_norm, kv_norm, w_uq, w_ukv,
              head_norm, w_out, norm_gains, mem_norm, wq_x, wkv_x, wo_x, w_up, conv_w, conv_b,
              w_down):
    for i in range(DEPTH):
        g = norm_gains[i]
        lam_init = 0.8 - 0.6 * math.exp(-0.3 * i)
        h = rmsnorm(x, g[0])
        y = hybrid_mixer(h, positions, rel_bias, w_in[i], b_forget[i], lam[i], lam_init,
                         q_norm[i], kv_norm[i], w_uq[i], w_ukv[i], head_norm[i], w_out[i])
        x = x + rmsnorm(y, g[1])
        mem_n = rmsnorm(mem, mem_norm[i])
        h = rmsnorm(x, g[2])
        x = x + rmsnorm(memory_xattn(h, mem_n, wq_x[i], wkv_x[i], wo_x[i]), g[3])
        h = rmsnorm(x, g[4])
        x = x + rmsnorm(conv_ffn(h, w_up[i], conv_w[i], conv_b[i], w_down[i]), g[5])
    return x


_drawn_inputs = setup_inputs


def setup_inputs(seed=0):
    import zlib

    import numpy as np

    out = dict(_drawn_inputs(seed))
    spreads = {}
    factors = {'conv_b': 2.82}
    for name, (base, spread) in spreads.items():
        noise = np.random.default_rng([zlib.crc32(name.encode()), seed]).standard_normal(out[name].shape)
        drawn = base * np.exp(spread * noise) if base else spread * noise
        out[name] = jnp.asarray(drawn.astype(out[name].dtype))
    for name, factor in factors.items():
        out[name] = (out[name] * factor).astype(out[name].dtype)
    return out
```

```python
from contextlib import ExitStack

import numpy as np
import concourse.bass as bass
from concourse import mybir

F32 = mybir.dt.float32
F32R = mybir.dt.float32r
BF16 = mybir.dt.bfloat16
I32 = mybir.dt.int32
ALU = mybir.AluOpType
ACT = mybir.ActivationFunctionType
AX = mybir.AxisListType.X

P = 128
D, SEQ, DEPTH = 2048, 256, 2
TB = SEQ // P
KC = D // P
H_A, DK_A, H_B, D_B, H_C = 4, 64, 6, 128, 6
Q_LORA, KV_LORA, D_NOPE, D_ROPE = 512, 256, 64, 32
D_FF, H_X, D_X, CHUNK = 4096, 4, 128, 64
DQ_C = D_NOPE + D_ROPE
EPS, NEG = 1e-6, -1e30
HEADS = H_A + H_B + H_C
HR = D_ROPE // 2
C_QA, C_KA, C_VA, C_QB, C_KB, C_VB = 0, 512, 1024, 1536, 2304, 3072
C_F, C_CQ, C_CKV = 3840, 3846, 4358

PW = 1024
RAW = 8
SPL = 4

W_IN_GROUPS = [
    ("cq", "nat", 8, 2, 512), ("ckv", "nat", 8, 2, KV_LORA + D_ROPE),
    ("qa0", "T", 4, 4, 256), ("qa1", "T", 4, 4, 256), ("ka0", "T", 4, 4, 256), ("ka1", "T", 4, 4, 256),
    ("uqa", "nat", 2, 2, 512), ("small", "nat", 4, 0, 0), ("ukv0", "nat", 1, 2, 512), ("ukv1", "nat", 1, 2, 512),
    ("va", "nat", 8, 2, 512), ("vbf", "nat", 8, 2, 256 + 2 * H_B),
    ("qb0", "T", 4, 4, 256), ("kb0", "T", 4, 4, 256), ("vb", "nat", 8, 2, 512),
    ("qb1", "T", 4, 4, 256), ("kb1", "T", 4, 4, 256), ("qb2", "T", 4, 4, 256), ("kb2", "T", 4, 4, 256),
]
N_IN = sum(g[2] for g in W_IN_GROUPS)
P_OUT = N_IN
P_MEMK = P_OUT + 32
P_WQ = P_MEMK + 8
P_MEMV = P_WQ + 8
P_WO = P_MEMV + 8
P_UP = P_WO + 8
UPG = 16
P_DOWN = P_UP + 8 * UPG
NPIECES = P_DOWN + 64
assert NPIECES % RAW == 0 and all(p % RAW == 0 for p in (P_OUT, P_MEMK, P_WQ, P_MEMV, P_WO, P_UP, P_DOWN))
G_OUT = len(W_IN_GROUPS)
G_MEMK, G_WQ, G_MEMV, G_WO, G_DOWN, NGROUPS = G_OUT + 4, G_OUT + 6, G_OUT + 8, G_OUT + 9, G_OUT + 13, G_OUT + 17
assert NGROUPS % 2 == 0

HEAD_ORDER = [0, 1, 2, 3, 10, 11, 12, 13, 14, 15, 4, 5, 6, 7, 8, 9]

CG0, CG2, CG4, CMEM, CHEAD, CQN, CKVN, CCONV = 0, 16, 32, 48, 64, 80, 84, 86
NCOL = CCONV + 16 * UPG
RLAM, RBF, RINIT = 0, 256, 256 + 2 * H_B
NROW = RINIT + 2

NEAR = [1, 2, 3, 4, 5, 6, 7, 8, 14, 23, 39, 64, 108, 182, 305]
SQ_DB = float(np.float32(np.sqrt(D_B)))

HEAD_SEQ = [("C", h) for h in range(H_C)] + [("A", h) for h in range(H_A)] + [("B", h) for h in range(H_B)]


def jobs_of(n):
    return [(n, m) for m in range(2 if HEAD_SEQ[n][0] == "A" else 1)]


JOB = {}
for _n in range(HEADS):
    for _j in jobs_of(_n):
        JOB[_j] = len(JOB)


def input_phase_steps():
    after = {}

    def at(p, *steps):
        after.setdefault(p, []).extend(steps)

    ends = {}
    p = 0
    for gi, (name, _, n, _, _) in enumerate(W_IN_GROUPS):
        p += n
        ends[name] = p - 1
        at(p - 1, ("evac", gi))
    at(ends["ckv"], ("latent_stats",))
    at(ends["qa0"] + 1, *[("latent_T", i) for i in range(5)])
    at(ends["ukv1"], ("rope_q",), ("k_cat",))
    at(ends["ukv1"] + 3, *[("latent_qk_T", h) for h in range(3)])
    at(ends["ukv1"] + 4, *[("latent_qk_T", h) for h in range(3, 6)])
    at(ends["vbf"], ("forget",), )
    at(ends["vbf"] + 1, ("forget_scan",))
    starts = [46, 48, 50, 52, 54, 56, 58, 61, 64, 67, 70, 72, 80, 82]
    for n, q in enumerate(starts):
        if n >= 2:
            at(q, ("O", n - 2))
        if n >= 1:
            at(q, ("T", n - 1))
        at(q, ("S", n))
        at(q + 1, ("N", n))
    at(84, ("onorm", 10, 16), ("onorm", 0, 4))
    steps = []
    for p in range(N_IN):
        steps.append(("mm", p))
        steps.append(("split", p + SPL))
        steps.extend(sorted(after.get(p, []), key=lambda s: s[0] != "evac"))
    n = len(starts)
    for q in range(n, HEADS + 2):
        steps.append(("O", q - 2))
        if q - 1 < HEADS:
            steps.append(("T", q - 1))
        if q < HEADS:
            steps += [("S", q), ("head_T", 2 * (q - n)), ("head_T", 2 * (q - n) + 1), ("N", q)]
        elif q == HEADS:
            steps.append(("head_T", 4))
    steps.append(("onorm", 4, 10))
    steps.extend(("head_T", i) for i in range(5, 8))
    return steps


STEPS = input_phase_steps()


def piece_group(p):
    for gi, (_, _, n, _, _) in enumerate(W_IN_GROUPS):
        if p < n:
            return gi, p
        p -= n


def piece_width(p):
    if p >= N_IN:
        return PW
    gi, j = piece_group(p)
    _, kind, _, ch, w = W_IN_GROUPS[gi]
    return P if ch == 0 else ch * w


def bank_items():
    items = [("h1", i) for i in range(8)]
    for s in STEPS:
        if s[0] in ("latent_T", "latent_qk_T", "head_T", "O", "T"):
            items.append(s)
        elif s[0] == "S":
            items += [("S", j) for j in jobs_of(s[1])]
        elif s[0] == "forget_scan":
            items.append(s)
    items += [("mem_T", i) for i in range(8)] + [("h2", i) for i in range(8)]
    items += [("XS", 0), ("XS", 1), ("XS", 2), ("XS", 3)]
    for h in range(H_X):
        items += [("XT", h), ("XO", h)]
    items += [("h3", i) for i in range(8)]
    assert len(items) % 4 == 0, len(items)
    return items


ITEMS = bank_items()
ITEM = {name: w for w, name in enumerate(ITEMS)}
assert len(ITEM) == len(ITEMS)
NITEMS = len(ITEMS)

GROUP = {g[0]: i for i, g in enumerate(W_IN_GROUPS)}
GROUP_END = {}
_p = 0
for _i, _g in enumerate(W_IN_GROUPS):
    _p += _g[2]
    GROUP_END[_i] = _p
for _i in range(4):
    GROUP_END[G_OUT + _i] = P_OUT + 8 * (_i + 1)
    GROUP_END[G_WO + _i] = P_WO + 2 * (_i + 1)
    GROUP_END[G_DOWN + _i] = P_DOWN + 16 * (_i + 1)
for _i in range(2):
    GROUP_END[G_MEMK + _i] = P_MEMK + 4 * (_i + 1)
    GROUP_END[G_WQ + _i] = P_WQ + 4 * (_i + 1)
GROUP_END[G_MEMV] = P_MEMV + 8
T_GROUPS = [i for i, g in enumerate(W_IN_GROUPS) if g[1] == "T"] + [G_MEMK, G_MEMK + 1, G_WQ, G_WQ + 1]
T_BEFORE = dict(zip(T_GROUPS, [None] + T_GROUPS))

LATENT_CHUNKS = [[0, 1], [2], [3], [4], [5]]
TSPLITS = ([("h1", i) for i in range(8)] + [("latent_T", i) for i in range(5)]
           + [("head_T", i) for i in range(8)] + [("mem_T", i) for i in range(8)]
           + [("h2", i) for i in range(8)] + [("XO", i) for i in range(4)] + [("h3", i) for i in range(8)])
TSPLIT = {name: n for n, name in enumerate(TSPLITS)}
NTSPLIT = len(TSPLITS)

RSTDS = ["h1", "latent", "o10", "o0", "o4", "y1", "h2", "y2", "h3", "y3"]
RSTD = {name: n for n, name in enumerate(RSTDS)}
NRSTD = len(RSTDS)

DVE_STEPS = 104
ACT_STEPS = 10


class Steps:

    def __init__(self, eng, sem):
        self.eng, self.sem, self.base, self.n = eng, sem, 0, 0

    def done(self, ins):
        ins.then_inc(self.sem, 1)
        self.n += 1
        self.eng.wait_ge(self.sem, self.base + self.n)


def build(nc, stream, x_in, mem_in, pos_in, posq_in, rel_in, cols_in, rows_in, gains_in, inv_in, out):
    with ExitStack() as ctx:
        def sem(name):
            return ctx.enter_context(nc.semaphore(name))

        base = (nc.sbuf_base + 31) // 32 * 32
        K = 1024

        def sb(name, shape, off, dt=F32):
            n = int(np.prod(shape[1:])) * (2 if dt == BF16 else 4)
            assert base + off + n <= nc.sbuf_usable_end, (name, off, n)
            return nc.alloc_sbuf_tensor_at(name, shape, dt, offset=base + off)

        raw = sb("raw", [P, RAW, PW], 0)
        w_hi = sb("w_hi", [P, SPL, PW], 32 * K, F32R)
        w_lo = sb("w_lo", [P, SPL, PW], 48 * K, F32R)
        x = sb("x", [P, TB, D], 64 * K)
        h_t = sb("h_t", [P, KC, 2, SEQ], 80 * K, F32R)
        BIG = 112 * K
        qa_t = sb("qa_t", [P, 4, SEQ], BIG)
        ka_t = sb("ka_t", [P, 4, SEQ], BIG + 4 * K)
        qb_t = sb("qb_t", [P, 6, SEQ], BIG + 8 * K)
        kb_t = sb("kb_t", [P, 6, SEQ], BIG + 14 * K)
        qc_t = sb("qc_t", [P, 6, SEQ], BIG + 20 * K)
        kc_t = sb("kc_t", [P, 6, SEQ], BIG + 26 * K)
        va = sb("va", [P, TB, 512], BIG + 32 * K)
        vb = sb("vb", [P, TB, 768], BIG + 36 * K)
        vc = sb("vc", [P, TB, 768], BIG + 42 * K)
        o_nat = sb("o_nat", [P, TB, D], BIG + 48 * K)
        sq_all = sb("sq_all", [P, TB, 6, P], BIG + 20 * K)
        cq = sb("cq", [P, TB, Q_LORA], BIG + 8 * K)
        ckv = sb("ckv", [P, TB, KV_LORA + D_ROPE], BIG + 12 * K)
        q_nat = sb("q_nat", [P, TB, H_C, DQ_C], BIG + 8 * K)
        k_cat = sb("k_cat", [P, TB, H_C, DQ_C], BIG + 12 * K + 768)
        rope_a = sb("rope_a", [P, TB, H_C, HR], BIG + 17 * K + 512)
        rope_b = sb("rope_b", [P, TB, H_C, HR], BIG + 18 * K + 256)
        rope_c = sb("rope_c", [P, TB, H_C, HR], BIG + 19 * K)
        c_t = sb("c_t", [P, 6, 2, SEQ], BIG + 48 * K, F32R)
        lf_ones = sb("lf_ones", [P, SEQ], BIG + 14 * K)
        f_row = sb("f_row", [P, SEQ], BIG + 15 * K)
        posk_i = sb("posk_i", [P, SEQ], BIG, I32)
        posk = sb("posk", [P, SEQ], BIG + K)
        rel = sb("rel", [P, 384], BIG + 32 * K)
        ind = sb("ind", [P, 384], BIG + 33 * K + 512)
        tab = sb("tab", [P, 32, H_A], BIG + 35 * K)
        dtab = sb("dtab", [P, 30, H_A], BIG + 35 * K + 512)
        btmp = sb("btmp", [P, H_A, 384], BIG + 36 * K)
        m_t = sb("m_t", [P, KC, 2, SEQ], BIG, F32R)
        y_a = sb("y_a", [P, TB, D], BIG + 32 * K)
        m_nat = sb("m_nat", [P, TB, D], BIG + 48 * K)
        kx_t = sb("kx_t", [P, H_X, SEQ], BIG + 48 * K)
        qx_t = sb("qx_t", [P, H_X, SEQ], BIG + 52 * K)
        vx = sb("vx", [P, TB, 512], BIG + 56 * K)
        px = sb("px", [P, 2, TB, SEQ], BIG + 60 * K)
        px_t = sb("px_t", [P, 2, 2, SEQ], BIG + 32 * K)
        px2 = sb("px2", [P, 2, TB, SEQ], BIG + 36 * K)
        xo_t = sb("xo_t", [P, 4, 2, SEQ], BIG, F32R)
        act_t = sb("act_t", [P, 2 * KC, 2, SEQ], BIG, F32R)
        y_f = sb("y_f", [P, TB, D], 80 * K)
        gain_f = sb("gain_f", [P, D], 96 * K)
        SCR = 176 * K
        s_sb = sb("s_sb", [P, 3, 384], SCR)
        p_t = sb("p_t", [P, 384], SCR + 4 * K + 512)
        fa = sb("fa", [P, SEQ], SCR + 6 * K)
        fb = sb("fb", [P, H_B, SEQ], SCR + 7 * K)
        t_lo = sb("t_lo", [P, 2, SEQ], SCR + 13 * K)
        gain_a = sb("gain_a", [P, D], SCR)
        junk = sb("junk", [P, D], SCR + 8 * K, BF16)
        t_lo2 = sb("t_lo2", [P, 2, SEQ], SCR + 13 * K)
        up_lo = sb("up_lo", [P, 4, SEQ], SCR)
        up_u = sb("up_u", [P, 4, SEQ], SCR + 4 * K)
        up_c = sb("up_c", [P, 4, SEQ], SCR + 8 * K)
        up_g = sb("up_g", [P, 2, SEQ], SCR + 12 * K)
        up_a = sb("up_a", [P, 2, SEQ], SCR + 14 * K)
        off = [192 * K]

        def small(name, shape, dt=F32):
            t = sb(name, shape, off[0], dt)
            off[0] += (int(np.prod(shape[1:])) * 4 + 31) // 32 * 32
            return t

        bias = small("bias", [P, H_A, 384])
        mask_b = small("mask_b", [P, 384])
        mask_c = small("mask_c", [P, 384])
        ident = small("ident", [P, P])
        diag = small("diag", [P, TB, P])
        diag_m = small("diag_m", [P, TB, P])
        cols = small("cols", [P, NCOL])
        rows = small("rows", [P, NROW])
        inv = small("inv", [P, HR])
        trig = small("trig", [P, 2, TB, HR])
        ang = small("ang", [P, TB, HR])
        kr = small("kr", [P, TB, D_ROPE])
        posq_i = small("posq_i", [P, TB], I32)
        posq = small("posq", [P, TB])
        ssq = small("ssq", [P, 32])
        var = small("var", [P, 32])
        rs0 = small("rs0", [P, 32])
        rst = small("rst", [P, 32])
        ysq = small("ysq", [P, TB, 4])
        lamv = small("lamv", [P, 8])
        nmax = small("nmax", [P, 4, TB])
        sums = small("sums", [P, 4, TB])
        rcp = small("rcp", [P, 4, TB])
        o_r = small("o_r", [P, TB, HEADS])
        o_sq = small("o_sq", [P, TB, HEADS])
        z_f = small("z_f", [P, TB, 2 * H_B])
        e_f = small("e_f", [P, TB, 2 * H_B])
        cw = small("cw", [P, 16])

        def sq_tile(h0, h1):
            return sq_all[:, :, 0:h1 - h0, :]

        ps = ctx.enter_context(nc.psum_tensor("ps", [P, 8, 512], F32))
        lam_prod = rope_a

        landed = [sem(f"landed{i}") for i in range(RAW)]
        hi_ready = sem("hi_ready")
        lo_ready = sem("lo_ready")
        split_free = sem("split_free")
        acc_free = [sem(f"acc_free{i}") for i in range(2)]
        t_lo_ready = sem("t_lo_ready")
        bank_done = sem("bank_done")
        bank_free = [sem(f"bank_free{i}") for i in range(4)]
        tsplit_hi = sem("tsplit_hi")
        x_ready = sem("x_ready")
        ssq_ready = sem("ssq_ready")
        var_ready = sem("var_ready")
        rs0_ready = sem("rs0_ready")
        diag_ready = sem("diag_ready")
        y_sq = sem("y_sq")
        y_gained = sem("y_gained")
        gain_here = sem("gain_here")
        par_here = sem("par_here")
        mem_here = sem("mem_here")
        first_here = sem("first_here")
        setup_pool = sem("setup_pool")
        setup_dve = sem("setup_dve")
        setup_act = sem("setup_act")
        tab_ready = sem("tab_ready")
        rst_ready = sem("rst_ready")
        up_tap = sem("up_tap")
        bias_done = sem("bias_done")
        diagm_ready = sem("diagm_ready")
        lam_prod_ready = sem("lam_prod_ready")
        lam_exp_ready = sem("lam_exp_ready")
        c_scaled = sem("c_scaled")
        k_cat_ready = sem("k_cat_ready")
        f_abs = sem("f_abs")
        f_exp = sem("f_exp")
        f_one = sem("f_one")
        f_ln = sem("f_ln")
        lf_ready = sem("lf_ready")
        fab_ready = sem("fab_ready")
        s_ready = sem("s_ready")
        p_ready = sem("p_ready")
        pn_ready = sem("pn_ready")
        osq_ready = sem("osq_ready")
        oscl_ready = sem("oscl_ready")
        on_ready = sem("on_ready")
        xm_ready = sem("xm_ready")
        xpn_ready = sem("xpn_ready")
        up_free = [sem(f"up_free{i}") for i in range(2)]
        up_lo_ready = sem("up_lo_ready")
        up_aff_ready = sem("up_aff_ready")
        up_conv_ready = sem("up_conv_ready")
        up_gelu_ready = sem("up_gelu_ready")
        up_mul_ready = sem("up_mul_ready")
        up_hi_ready = sem("up_hi_ready")
        act_ready = sem("act_ready")
        cw_ready = sem("cw_ready")
        gate = sem("gate")
        stored = sem("stored")
        dve_step = sem("dve_step")
        act_step = sem("act_step")
        pool_step = sem("pool_step")

        def acc_read(l, g):
            return acc_free[g % 2], l * (NGROUPS // 2) + (g // 2 + 2)

        def item_read(l, item):
            w = ITEM[item]
            return bank_free[w % 4], l * (NITEMS // 4) + (w // 4 + 2)

        def pieces_used(l, p):
            return split_free, l * NPIECES + (SPL + p)

        def score_tile_slot(n):
            return JOB[(n, 0)] % 3

        def acc(g, b):
            return ps[:, 2 * (g % 2) + b, :]

        def bank(item):
            return ps[:, 4 + ITEM[item] % 4, :]

        def tsplit_job(item):
            kind, i = item
            if kind in ("h1", "h2", "h3"):
                g0 = {"h1": CG0, "h2": CG2, "h3": CG4}[kind]
                return h_t, [2 * i, 2 * i + 1], [g0 + 2 * i, g0 + 2 * i + 1]
            if kind == "mem_T":
                return m_t, [2 * i, 2 * i + 1], [CMEM + 2 * i, CMEM + 2 * i + 1]
            if kind == "head_T":
                return h_t, [2 * i, 2 * i + 1], [CHEAD + HEAD_ORDER[2 * i], CHEAD + HEAD_ORDER[2 * i + 1]]
            if kind == "latent_T":
                return c_t, LATENT_CHUNKS[i], [CQN + c for c in LATENT_CHUNKS[i]]
            return xo_t, [i], None

        block = ctx.enter_context(nc.Block())

        @block.sync
        def _(sp):
            sp.dma_start(x[:], x_in.rearrange("(t p) d -> p t d", p=P)).then_inc(first_here, 16)
            for j in range(RAW):
                sp.dma_start(raw[:, j, :], stream[j]).then_inc(landed[j], 16)
            with sp.Fori(1, DEPTH * NPIECES // RAW) as r:
                for j in range(RAW):
                    sp.wait_ge(lo_ready, r * RAW + (j + 1 - RAW))
                    sp.dma_start(raw[:, j, :], stream[r * RAW + j]).then_inc(landed[j], 16)
            for j in range(SPL):
                sp.wait_ge(lo_ready, DEPTH * NPIECES + j + 1 - RAW)
                sp.dma_start(raw[:, j, :], stream[DEPTH * NPIECES + j]).then_inc(landed[j], 16)
            for j in range(SPL):
                sp.wait_ge(landed[j], 16 * (DEPTH * NPIECES // RAW + 1))

        @block.tensor
        def _(pe):
            pe.sem_inc(split_free, SPL)

            with pe.Fori(0, DEPTH) as l:
                def take_bank(item):
                    w = ITEM[item]
                    pe.wait_ge(bank_free[w % 4], l * (NITEMS // 4) + w // 4 + 1)
                    return bank(item)

                def take_acc(g, g_count=None):
                    pe.wait_ge(acc_free[g % 2], l * (NGROUPS // 2) + (g // 2 + 1 if g_count is None else g_count))

                def take_piece(p):
                    pe.wait_ge(lo_ready, l * NPIECES + p + 1)

                def nat_mm(g, slot, c0, src, chunks, width, first, last, col=0, woff=0):
                    hi = w_hi[:, slot, woff:woff + len(chunks) * width].rearrange("p (c n) -> p c n", n=width)
                    lo = w_lo[:, slot, woff:woff + len(chunks) * width].rearrange("p (c n) -> p c n", n=width)
                    for j, c in enumerate(chunks):
                        f, e = first and j == 0, last and j == len(chunks) - 1
                        for tb in range(TB):
                            dst = acc(g, tb)[:, col:col + width]
                            s_hi = src[:, c, 0, tb * P:(tb + 1) * P]
                            s_lo = src[:, c, 1, tb * P:(tb + 1) * P]
                            pe.matmul(dst, s_hi, hi[:, j, :], start=f, stop=False, skip_group_check=True)
                            pe.matmul(dst, s_hi, lo[:, j, :], start=False, stop=False, skip_group_check=True)
                            mm = pe.matmul(dst, s_lo, hi[:, j, :], start=False, stop=e, skip_group_check=True)
                    return mm

                def t_mm(g, slot, src, chunks, first, last):
                    hi = w_hi[:, slot, :].rearrange("p (c n) -> p c n", n=256)
                    lo = w_lo[:, slot, :].rearrange("p (c n) -> p c n", n=256)
                    for j, c in enumerate(chunks):
                        f, e = first and j == 0, last and j == len(chunks) - 1
                        for nt in range(2):
                            dst = acc(g, nt)
                            pe.matmul(dst, hi[:, j, nt * P:(nt + 1) * P], src[:, c, :, :],
                                      start=f, stop=False, skip_group_check=True)
                            mm = pe.matmul(dst[:, SEQ:2 * SEQ], lo[:, j, nt * P:(nt + 1) * P], src[:, c, 0, :],
                                           start=False, stop=e, skip_group_check=True)
                    return mm

                def tile_ready(item):
                    pe.wait_ge(*item_read(l, item))

                def diag_transposes(kind, src, dg):
                    for i in range(8):
                        b = take_bank((kind, i))
                        for kk in range(2):
                            for tb in range(TB):
                                mm = pe.matmul(b[:, kk * SEQ + tb * P:kk * SEQ + (tb + 1) * P],
                                               src[:, tb, (2 * i + kk) * P:(2 * i + kk + 1) * P], dg[:, tb, :],
                                               start=True, stop=True)
                        mm.then_inc(bank_done, 1)

                def w_in_piece(p):
                    gi, j = piece_group(p)
                    name, kind, n, ch, width = W_IN_GROUPS[gi]
                    if j == 0:
                        take_acc(gi)
                    take_piece(p)
                    if kind == "T":
                        mm = t_mm(gi, p % SPL, h_t, range(4 * j, 4 * j + 4), j == 0, j == n - 1)
                    elif name == "uqa":
                        tile_ready(("latent_T", 2))
                        mm = nat_mm(gi, p % SPL, 0, c_t, [2 * j, 2 * j + 1], 512, j == 0, j == 1)
                    elif name == "small":
                        tile_ready(("latent_T", 4))
                        if j < 2:
                            mm = nat_mm(gi, p % SPL, 0, c_t, [2 * j, 2 * j + 1], 64, j == 0, j == 1)
                        else:
                            mm = nat_mm(gi, p % SPL, 0, c_t, [2 + j], 128, j == 2, j == 3, col=64)
                    elif name.startswith("ukv"):
                        mm = nat_mm(gi, p % SPL, 0, c_t, [4, 5], 512, True, True)
                    else:
                        if gi == 0:
                            tile_ready(("h1", j))
                        mm = nat_mm(gi, p % SPL, 0, h_t, [2 * j, 2 * j + 1], width, j == 0, j == n - 1)
                    mm.then_inc(split_free, 1)

                pe.wait_ge(diag_ready, l * 3 + 1)
                diag_transposes("h1", x, diag)

                for step in STEPS:
                    kind = step[0]
                    if kind == "mm":
                        w_in_piece(step[1])
                    elif kind == "latent_T":
                        pe.wait_ge(c_scaled, l + 1)
                        b = take_bank(step)
                        for kk, c in enumerate(LATENT_CHUNKS[step[1]]):
                            src = cq[:, :, c * P:(c + 1) * P] if c < 4 else ckv[:, :, (c - 4) * P:(c - 3) * P]
                            for tb in range(TB):
                                mm = pe.transpose(b[:, kk * SEQ + tb * P:kk * SEQ + (tb + 1) * P], src[:, tb, :], ident[:])
                        mm.then_inc(bank_done, 1)
                    elif kind == "latent_qk_T":
                        h = step[1]
                        pe.wait_ge(k_cat_ready, l + 1)
                        b = take_bank(step)
                        for a, src in enumerate((q_nat, k_cat)):
                            for tb in range(TB):
                                mm = pe.transpose(b[0:DQ_C, a * SEQ + tb * P:a * SEQ + (tb + 1) * P], src[:, tb, h, :], ident[:])
                        mm.then_inc(bank_done, 1)
                    elif kind == "forget_scan":
                        pe.wait_ge(lf_ready, l + 1)
                        b = take_bank(step)
                        for tb in range(TB):
                            mm = pe.transpose(b[0:2 * H_B, tb * P:(tb + 1) * P], z_f[:, tb, :], ident[:])
                        mm.then_inc(bank_done, 1)
                    elif kind == "S":
                        hk, h = HEAD_SEQ[step[1]]
                        if hk == "A":
                            pe.wait_ge(*acc_read(l, GROUP[f"qa{h // 2}"]))
                            pe.wait_ge(*acc_read(l, GROUP[f"ka{h // 2}"]))
                        elif hk == "B":
                            pe.wait_ge(*acc_read(l, GROUP[f"qb{h // 2}"]))
                            pe.wait_ge(*acc_read(l, GROUP[f"kb{h // 2}"]))
                            pe.wait_ge(fab_ready, l + 1)
                        else:
                            pe.wait_ge(*item_read(l, ("latent_qk_T", h)))
                        for job in jobs_of(step[1]):
                            b = take_bank(("S", job))
                            m = job[1]
                            for tb, (o, nk) in enumerate(((0, P), (P, SEQ))):
                                dst, q = b[:, o:o + nk], slice(tb * P, (tb + 1) * P)
                                if hk == "A":
                                    r = slice(m * DK_A, (m + 1) * DK_A)
                                    mm = pe.matmul(dst, qa_t[r, h, q], ka_t[r, h, 0:nk], start=True, stop=True)
                                elif hk == "B":
                                    pe.matmul(dst, qb_t[:, h, q], kb_t[:, h, 0:nk], start=True, stop=False)
                                    mm = pe.matmul(dst, fa[0:2 * H_B, q], fb[0:2 * H_B, h, 0:nk], start=False, stop=True)
                                else:
                                    mm = pe.matmul(dst, qc_t[0:DQ_C, h, q], kc_t[0:DQ_C, h, 0:nk], start=True, stop=True)
                            mm.then_inc(bank_done, 1)
                    elif kind == "T":
                        n = step[1]
                        slot = score_tile_slot(n)
                        if HEAD_SEQ[n][0] == "A":
                            pe.wait_ge(pn_ready, l * H_A + HEAD_SEQ[n][1] + 1)
                        else:
                            pe.wait_ge(p_ready, l * len(JOB) + JOB[(n, 0)] + 1)
                        b = take_bank(step)
                        for t, o in enumerate((0, P, 2 * P)):
                            mm = pe.transpose(b[:, t * P:(t + 1) * P], s_sb[:, slot, o:o + P], ident[:])
                        mm.then_inc(bank_done, 1)
                    elif kind == "O":
                        n = step[1]
                        hk, h = HEAD_SEQ[n]
                        v = {"A": va, "B": vb, "C": vc}[hk]
                        for name in {"A": ["va"], "B": ["vb", "vbf"], "C": ["small", "ukv0", "ukv1"]}[hk]:
                            pe.wait_ge(*acc_read(l, GROUP[name]))
                        pe.wait_ge(*item_read(l, ("T", n)))
                        b = take_bank(step)
                        vh = v[:, :, h * P:(h + 1) * P]
                        pe.matmul(b[:, 0:P], p_t[:, 0:P], vh[:, 0, :], start=True, stop=True)
                        pe.matmul(b[:, P:2 * P], p_t[:, P:2 * P], vh[:, 0, :], start=True, stop=False, skip_group_check=True)
                        mm = pe.matmul(b[:, P:2 * P], p_t[:, 2 * P:3 * P], vh[:, 1, :], start=False, stop=True,
                                       skip_group_check=True)
                        mm.then_inc(bank_done, 1)
                    elif kind == "head_T":
                        i = step[1]
                        pe.wait_ge(on_ready, l * 3 + (2 if i < 5 else 3))
                        b = take_bank(step)
                        for kk in range(2):
                            h = HEAD_ORDER[2 * i + kk]
                            for tb in range(TB):
                                mm = pe.transpose(b[:, kk * SEQ + tb * P:kk * SEQ + (tb + 1) * P],
                                                  o_nat[:, tb, h * P:(h + 1) * P], ident[:])
                        mm.then_inc(bank_done, 1)

                def nat_group(g, slot0, p, src, kc, item_kind=None, g_count=None, pp=2):
                    take_acc(g, g_count)
                    for j in range(kc // pp):
                        take_piece(p + j)
                        if item_kind is not None:
                            tile_ready((item_kind, j))
                        mm = nat_mm(g, (slot0 + j) % SPL, 0, src, [2 * j, 2 * j + 1], 512, j == 0, j == kc // pp - 1)
                        mm.then_inc(split_free, 1)

                def t_group(g, p, src, last_item):
                    take_acc(g)
                    for j in range(4):
                        take_piece(p + j)
                        if last_item is not None:
                            for k in range(2):
                                tile_ready((last_item, 2 * j + k))
                        t_mm(g, (p + j) % SPL, src, range(4 * j, 4 * j + 4), j == 0, j == 3).then_inc(split_free, 1)

                with pe.Fori(0, 2) as i:
                    for k in range(2):
                        g = G_OUT + k
                        nat_group(g, 0, i * 16 + (P_OUT + 8 * k), h_t, KC, "head_T",
                                  g_count=i + ((G_OUT + k) // 2 + 1))
                pe.wait_ge(mem_here, l * 16 + 32)
                pe.wait_ge(diagm_ready, 1)
                diag_transposes("mem_T", m_nat, diag_m)
                for k in range(2):
                    t_group(G_MEMK + k, P_MEMK + 4 * k, m_t, "mem_T" if k == 0 else None)
                pe.wait_ge(diag_ready, l * 3 + 2)
                diag_transposes("h2", x, diag)
                for k in range(2):
                    t_group(G_WQ + k, P_WQ + 4 * k, h_t, "h2" if k == 0 else None)
                for h in range(H_X):
                    pe.wait_ge(*acc_read(l, G_MEMK + h // 2))
                    pe.wait_ge(*acc_read(l, G_WQ + h // 2))
                    b = take_bank(("XS", h))
                    for tb in range(TB):
                        mm = pe.matmul(b[:, tb * SEQ:(tb + 1) * SEQ], qx_t[:, h, tb * P:(tb + 1) * P], kx_t[:, h, :],
                                       start=True, stop=True)
                    mm.then_inc(bank_done, 1)
                nat_group(G_MEMV, 0, P_MEMV, m_t, KC)
                pe.wait_ge(*acc_read(l, G_MEMV))
                for h in range(H_X):
                    pe.wait_ge(xpn_ready, l * H_X + h + 1)
                    b = take_bank(("XT", h))
                    for kb in range(2):
                        for tb in range(TB):
                            mm = pe.transpose(b[:, kb * SEQ + tb * P:kb * SEQ + (tb + 1) * P],
                                              (px if h < 2 else px2)[:, h % 2, tb, kb * P:(kb + 1) * P], ident[:])
                    mm.then_inc(bank_done, 1)
                    pe.wait_ge(*item_read(l, ("XT", h)))
                    b = take_bank(("XO", h))
                    for kb in range(2):
                        mm = pe.matmul(b[:, 0:SEQ], vx[:, kb, h * P:(h + 1) * P], px_t[:, h % 2, kb, :],
                                       start=(kb == 0), stop=(kb == 1))
                    mm.then_inc(bank_done, 1)
                for k in range(4):
                    g = G_WO + k
                    take_acc(g)
                    for j in range(2):
                        take_piece(P_WO + 2 * k + j)
                        tile_ready(("XO", 2 * j + 1))
                        nat_mm(g, (2 * k + j) % SPL, 0, xo_t, [2 * j, 2 * j + 1], 512, j == 0, j == 1).then_inc(split_free, 1)
                pe.wait_ge(diag_ready, l * 3 + 3)
                diag_transposes("h3", x, diag)
                for s in range(2):
                    pe.wait_ge(acc_free[s], l * (NGROUPS // 2) + (G_DOWN - s + 1) // 2 + 1)
                for b in range(4):
                    pe.wait_ge(bank_free[b], l * (NITEMS // 4) + NITEMS // 4 + 1)
                pe.sem_inc(gate, 1)
                with pe.Fori(0, UPG // 2) as i:
                    for half in range(2):
                        pe.wait_ge(up_free[half], l * (UPG // 2) + i + 1)
                        for j in range(8):
                            take_piece(i * 16 + (P_UP + 8 * half + j))
                            tile_ready(("h3", j))
                            hi = w_hi[:, j % SPL, :].rearrange("p (c n) -> p c n", n=512)
                            lo = w_lo[:, j % SPL, :].rearrange("p (c n) -> p c n", n=512)
                            for cc in range(2):
                                c = 2 * j + cc
                                for nt in range(4):
                                    dst = ps[:, 4 * half + nt, :]
                                    pe.matmul(dst, hi[:, cc, nt * P:(nt + 1) * P], h_t[:, c, :, :],
                                              start=(c == 0), stop=False, skip_group_check=True)
                                    mm = pe.matmul(dst[:, SEQ:2 * SEQ], lo[:, cc, nt * P:(nt + 1) * P], h_t[:, c, 0, :],
                                                   start=False, stop=(c == KC - 1), skip_group_check=True)
                            mm.then_inc(split_free, 1)
                pe.wait_ge(up_free[0], l * (UPG // 2) + UPG // 2 + 1)
                pe.sem_inc(gate, 1)
                with pe.Fori(0, 2) as i:
                    for k in range(2):
                        g = G_DOWN + k
                        take_acc(g, i + (g // 2 + 1))
                        for j in range(16):
                            take_piece(i * 32 + (P_DOWN + 16 * k + j))
                            if k == 0:
                                pe.wait_ge(act_ready, l * UPG + j + 1)
                            nat_mm(g, j % SPL, 0, act_t, [2 * j, 2 * j + 1], 512, j == 0, j == 15).then_inc(split_free, 1)
                pe.wait_ge(up_free[1], l * (UPG // 2) + UPG // 2 + 1)
                pe.sem_inc(gate, 1)
    
        @block.scalar
        def _(act):
            st = Steps(act, act_step)

            def split_hi(slot, rslot, landed_count, piece_count, width=PW):
                act.wait_ge(landed[rslot], landed_count)
                act.wait_ge(split_free, piece_count)
                act.activation(w_hi[:, slot, 0:width], raw[:, rslot, 0:width], ACT.Copy).then_inc(hi_ready, 1)

            act.dma_start(posk_i[:], pos_in.partition_broadcast(P)).then_inc(first_here, 16)
            act.dma_start(posq_i[:], posq_in).then_inc(first_here, 16)
            act.dma_start(tab[:], rel_in.rearrange("b h -> (b h)").partition_broadcast(P)).then_inc(first_here, 16)
            act.dma_start(inv[:], inv_in.partition_broadcast(P)).then_inc(first_here, 16)
            act.dma_start(m_nat[:], mem_in.rearrange("(t p) d -> p t d", p=P)).then_inc(mem_here, 16)
            for p in range(SPL):
                split_hi(p, p, 16, p + 1, piece_width(p))
            act.wait_ge(setup_dve, 1)
            act.activation(trig[:], trig[:], ACT.Sin).then_inc(setup_act, 1)
            act.wait_ge(mem_here, 16)
            st.done(act.activation(junk[:], m_nat[:, 0, :], ACT.Square, accum_out=ssq[:, 0:1]))
            act.activation(junk[:], m_nat[:, 1, :], ACT.Square, accum_out=ssq[:, 1:2]).then_inc(setup_act, 1)
            act.wait_ge(setup_dve, 2)
            st.done(act.activation(rs0[:, 0:TB], var[:, 0:TB], ACT.Ln))
            act.activation(rs0[:, 0:TB], rs0[:, 0:TB], ACT.Exp, scale=-0.5).then_inc(setup_act, 1)
            SET = st.n

            with act.Fori(0, DEPTH) as l:
                st.base, st.n = l * ACT_STEPS + SET, 0

                def split(p):
                    w = piece_width(p % NPIECES)
                    split_hi(p % SPL, p % RAW, (l * (NPIECES // RAW) + p // RAW + 1) * 16, l * NPIECES + p + 1, w)

                def split_dyn(p0, j, i, per):
                    q = p0 + j
                    split_hi(q % SPL, q % RAW, (l * (NPIECES // RAW) + i * (per // RAW) + (q // RAW + 1)) * 16,
                             l * NPIECES + i * per + (q + 1))

                def read_bank(item):
                    act.wait_ge(bank_done, l * NITEMS + ITEM[item] + 1)
                    return bank(item)

                def free_bank(ins, item):
                    ins.then_inc(bank_free[ITEM[item] % 4], 1)

                def tsplit(item):
                    dst, chunks, gains = tsplit_job(item)
                    b = read_bank(item)
                    for kk, c in enumerate(chunks):
                        kw = {} if gains is None else {"scale": cols[:, gains[kk]:gains[kk] + 1]}
                        ins = act.activation(dst[:, c, 0, :], b[:, kk * SEQ:(kk + 1) * SEQ], ACT.Copy, **kw)
                    ins.then_inc(tsplit_hi, 1)

                def group_done(g, dyn=0):
                    act.wait_ge(*pieces_used(l, dyn + GROUP_END[g]))

                def rsqrt(name, a, b):
                    act.wait_ge(var_ready, l * NRSTD + RSTD[name] + 1)
                    st.done(act.activation(rs0[:, a:b], var[:, a:b], ACT.Ln))
                    act.activation(rs0[:, a:b], rs0[:, a:b], ACT.Exp, scale=-0.5).then_inc(rs0_ready, 1)

                def x_stats(k):
                    for tb in range(TB):
                        act.wait_ge(x_ready, (l * 3 + k) * TB + tb + 1)
                        ins = act.activation(junk[:], x[:, tb, :], ACT.Square, accum_out=ssq[:, tb:tb + 1])
                        ins.then_inc(ssq_ready, 1)
                        act.wait_ge(ssq_ready, l * 7 + (0, 3, 5)[k] + tb + 1)

                def t_evac_lo(g):
                    group_done(g)
                    if T_BEFORE[g] is not None:
                        act.wait_ge(*acc_read(l, T_BEFORE[g]))
                    act.activation(t_lo[:], ps[:, 2 * (g % 2):2 * (g % 2) + 2, SEQ:2 * SEQ], ACT.Copy).then_inc(t_lo_ready, 1)

                def nat_evac(g, dsts):
                    group_done(g)
                    for dst, tb, a, b in dsts:
                        ins = act.activation(dst, acc(g, tb)[:, a:b], ACT.Copy)
                    ins.then_inc(acc_free[g % 2], 1)

                def y_evac(g, yt, o, ssq_col, dyn=0, passes=0):
                    group_done(g, dyn)
                    for tb in range(TB):
                        ins = act.activation(yt[:, tb, bass.ds(o, 512)], acc(g, tb), ACT.Copy)
                    ins.then_inc(acc_free[g % 2], 1)
                    act.wait_ge(acc_free[g % 2], l * (NGROUPS // 2) + passes + (g // 2 + 2))
                    for tb in range(TB):
                        ins = act.activation(junk[:, 512 * tb:512 * tb + 512], yt[:, tb, bass.ds(o, 512)], ACT.Square,
                                             accum_out=ysq[:, tb, bass.ds(ssq_col, 1)])
                    ins.then_inc(y_sq, 1)

                act.wait_ge(x_ready, l * 3 * TB + TB)
                act.dma_start(cols[:], cols_in[l]).then_inc(par_here, 16)
                act.dma_start(rows[:], rows_in[l].partition_broadcast(P)).then_inc(par_here, 16)
                x_stats(0)
                rsqrt("h1", 0, TB)
                act.wait_ge(lam_prod_ready, l + 1)
                act.activation(lamv[:, 2:4], lamv[:, 0:2], ACT.Exp).then_inc(lam_exp_ready, 1)
                act.wait_ge(par_here, l * 32 + 32)
                for i in range(8):
                    tsplit(("h1", i))

                for step in STEPS:
                    kind = step[0]
                    if kind == "split":
                        split(step[1])
                    elif kind == "evac":
                        gi = step[1]
                        name = W_IN_GROUPS[gi][0]
                        if W_IN_GROUPS[gi][1] == "T":
                            t_evac_lo(gi)
                            continue
                        group_done(gi)
                        if name == "va":
                            act.wait_ge(bias_done, 1)
                        moves = []
                        for tb in range(TB):
                            a = acc(gi, tb)
                            if name == "cq":
                                moves.append((cq[:, tb, :], a[:, 0:512]))
                            elif name == "ckv":
                                moves.append((ckv[:, tb, :], a[:, 0:288]))
                            elif name == "uqa":
                                moves.append((q_nat[:, tb].rearrange("p h d -> p (h d)")[:, 0:512], a[:, 0:512]))
                            elif name == "small":
                                moves.append((q_nat[:, tb].rearrange("p h d -> p (h d)")[:, 512:576], a[:, 0:64]))
                                moves.append((vc[:, tb, 640:768], a[:, 64:192]))
                            elif name == "ukv0":
                                kv = a[:, 0:384].rearrange("p (h d) -> p h d", d=192)
                                moves.append((k_cat[:, tb, 0:2, 0:64], kv[:, :, 0:64]))
                                moves.append((vc[:, tb, 0:256].rearrange("p (h d) -> p h d", d=P), kv[:, :, 64:192]))
                                moves.append((k_cat[:, tb, 2, 0:64], a[:, 384:448]))
                                moves.append((vc[:, tb, 256:320], a[:, 448:512]))
                            elif name == "ukv1":
                                moves.append((vc[:, tb, 320:384], a[:, 0:64]))
                                kv = a[:, 64:448].rearrange("p (h d) -> p h d", d=192)
                                moves.append((k_cat[:, tb, 3:5, 0:64], kv[:, :, 0:64]))
                                moves.append((vc[:, tb, 384:640].rearrange("p (h d) -> p h d", d=P), kv[:, :, 64:192]))
                                moves.append((k_cat[:, tb, 5, 0:64], a[:, 448:512]))
                            elif name == "va":
                                moves.append((va[:, tb, :], a[:, 0:512]))
                            elif name == "vbf":
                                moves.append((vb[:, tb, 512:768], a[:, 0:256]))
                                moves.append((z_f[:, tb, :], a[:, 256:256 + 2 * H_B]))
                            elif name == "vb":
                                moves.append((vb[:, tb, 0:512], a[:, 0:512]))
                        for dst, src in moves:
                            ins = act.activation(dst, src, ACT.Copy)
                        ins.then_inc(acc_free[gi % 2], 1)
                    elif kind == "latent_stats":
                        act.wait_ge(*acc_read(l, GROUP["ckv"]))
                        for tb in range(TB):
                            act.activation(junk[:, tb * 512:tb * 512 + 512], cq[:, tb, :], ACT.Square, accum_out=ssq[:, tb:tb + 1])
                        for tb in range(TB):
                            ins = act.activation(junk[:, 1024 + tb * 256:1280 + tb * 256], ckv[:, tb, 0:256], ACT.Square,
                                                 accum_out=ssq[:, 2 + tb:3 + tb])
                        ins.then_inc(ssq_ready, 1)
                        rsqrt("latent", 0, 4)
                        act.wait_ge(rst_ready, l + 1)
                        for tb in range(TB):
                            act.activation(cq[:, tb, :], cq[:, tb, :], ACT.Copy, scale=rst[:, tb:tb + 1])
                        for tb in range(TB):
                            ins = act.activation(ckv[:, tb, 0:256], ckv[:, tb, 0:256], ACT.Copy, scale=rst[:, 2 + tb:3 + tb])
                        ins.then_inc(c_scaled, 1)
                    elif kind == "latent_T":
                        tsplit(step)
                    elif kind == "latent_qk_T":
                        h = step[1]
                        b = read_bank(step)
                        act.activation(qc_t[0:DQ_C, h, :], b[0:DQ_C, 0:SEQ], ACT.Copy)
                        free_bank(act.activation(kc_t[0:DQ_C, h, :], b[0:DQ_C, SEQ:2 * SEQ], ACT.Copy), step)
                    elif kind == "forget":
                        act.wait_ge(f_abs, l + 1)
                        act.activation(e_f[:], e_f[:], ACT.Exp, scale=-1.0).then_inc(f_exp, 1)
                        act.wait_ge(f_one, l + 1)
                        act.activation(e_f[:], e_f[:], ACT.Ln).then_inc(f_ln, 1)
                    elif kind == "S":
                        for job in jobs_of(step[1]):
                            j = JOB[job]
                            act.wait_ge(s_ready, l * len(JOB) + j + 1)
                            for tb, (o, nk) in enumerate(((0, P), (P, SEQ))):
                                ins = act.activation(s_sb[:, j % 3, o:o + nk], s_sb[:, j % 3, o:o + nk], ACT.Exp,
                                                     bias=nmax[:, j % 4, tb:tb + 1], accum_out=sums[:, j % 4, tb:tb + 1])
                            ins.then_inc(p_ready, 1)
                    elif kind == "T":
                        n = step[1]
                        b = read_bank(step)
                        if n >= 1:
                            act.wait_ge(bank_done, l * NITEMS + ITEM[("O", n - 1)] + 1)
                        free_bank(act.activation(p_t[:], b[:, 0:384], ACT.Copy), step)
                    elif kind == "onorm":
                        h0, h1 = step[1:]
                        n = TB * (h1 - h0)
                        rsqrt(f"o{h0}", 0, n)
                    elif kind == "head_T":
                        if step[1] == 0:
                            group_done(G_OUT - 1)
                        tsplit(step)

                act.wait_ge(on_ready, l * 3 + 3)
                act.dma_start(gain_a[:], gains_in[l * 3].partition_broadcast(P)).then_inc(gain_here, 16)
                act.wait_ge(bank_done, l * NITEMS + ITEM[("head_T", 7)] + 1)
                act.dma_start(m_nat[:], mem_in.rearrange("(t p) d -> p t d", p=P)).then_inc(mem_here, 16)
                with act.Fori(0, 2) as i:
                    for k in range(2):
                        for j in range(8):
                            split_dyn(P_OUT + 8 * k + SPL, j, i, 16)
                        y_evac(G_OUT + k, y_a, i * 1024 + 512 * k, i * 2 + k, dyn=i * 16, passes=i)
                for i in range(8):
                    tsplit(("mem_T", i))
                rsqrt("y1", 0, TB)
                x_stats(1)
                rsqrt("h2", 0, TB)
                for k in range(2):
                    for j in range(4):
                        split(P_MEMK + 4 * k + SPL + j)
                    t_evac_lo(G_MEMK + k)
                for i in range(8):
                    tsplit(("h2", i))
                for k in range(2):
                    for j in range(4):
                        split(P_WQ + 4 * k + SPL + j)
                    t_evac_lo(G_WQ + k)
                act.dma_start(gain_a[:], gains_in[l * 3 + 1].partition_broadcast(P)).then_inc(gain_here, 16)
                for h in range(H_X):
                    act.wait_ge(xm_ready, l * H_X + h + 1)
                    b = bank(("XS", h))
                    for tb in range(TB):
                        ins = act.activation((px if h < 2 else px2)[:, h % 2, tb, :], b[:, tb * SEQ:(tb + 1) * SEQ], ACT.Exp,
                                             bias=nmax[:, h, tb:tb + 1], scale=float(D_X ** -0.5),
                                             accum_out=sums[:, h, tb:tb + 1])
                    free_bank(ins, ("XS", h))
                for j in range(8):
                    split(P_MEMV + SPL + j)
                nat_evac(G_MEMV, [(vx[:, tb, :], tb, 0, 512) for tb in range(TB)])
                for h in range(H_X):
                    b = read_bank(("XT", h))
                    if h >= 2:
                        act.wait_ge(bank_done, l * NITEMS + ITEM[("XO", h - 2)] + 1)
                    free_bank(act.activation(px_t[:, h % 2].rearrange("p a b -> p (a b)"), b, ACT.Copy), ("XT", h))
                    tsplit(("XO", h))
                for k in range(4):
                    for j in range(2):
                        split(P_WO + 2 * k + SPL + j)
                    y_evac(G_WO + k, y_a, 512 * k, k)
                rsqrt("y2", 0, TB)
                x_stats(2)
                rsqrt("h3", 0, TB)
                for i in range(8):
                    tsplit(("h3", i))

                def up_split(i, half, j):
                    split_dyn(P_UP + 8 * half + SPL, j, i, 16)

                def up_tail(i, half, j):
                    g = i * 2 + half
                    if j == 0:
                        act.wait_ge(*pieces_used(l, i * 16 + (P_UP + 8 * half + 8)))
                        act.wait_ge(up_free[1 - half], l * (UPG // 2) + i + (1 + half))
                        act.activation(up_lo[:], ps[:, 4 * half:4 * half + 4, SEQ:2 * SEQ], ACT.Copy).then_inc(up_lo_ready, 1)
                    if j == 3:
                        act.wait_ge(up_conv_ready, l * UPG + g + 1)
                        act.activation(up_g[:], up_c[:, 0:2, :], ACT.Gelu_apprx_tanh).then_inc(up_gelu_ready, 1)
                    if j == 5:
                        act.wait_ge(up_mul_ready, l * UPG + g + 2)
                        act.activation(act_t[:, bass.ds(2 * g, 2), 0, :], up_a[:], ACT.Copy).then_inc(up_hi_ready, 1)

                for j in range(8):
                    up_split(0, 0, j)
                with act.Fori(0, UPG // 2 - 1) as i:
                    for j in range(8):
                        up_split(i, 1, j)
                        up_tail(i, 0, j)
                    for j in range(8):
                        split_dyn(P_UP + 16 + SPL, j, i, 16)
                        up_tail(i, 1, j)
                for j in range(8):
                    up_split(UPG // 2 - 1, 1, j)
                    up_tail(UPG // 2 - 1, 0, j)
                for j in range(8):
                    split(P_DOWN + SPL + j)
                    up_tail(UPG // 2 - 1, 1, j)
                act.dma_start(gain_f[:], gains_in[l * 3 + 2].partition_broadcast(P)).then_inc(gain_here, 16)
                for j in range(8, 16):
                    split(P_DOWN + SPL + j)
                y_evac(G_DOWN, y_f, 0, 0)
                for k in range(1, 4):
                    for j in range(16):
                        split(P_DOWN + 16 * k + SPL + j)
                    y_evac(G_DOWN + k, y_f, 512 * k, k)
                rsqrt("y3", 0, TB)
                assert st.n == ACT_STEPS, ("ACT_STEPS", st.n)

            act.wait_ge(x_ready, (DEPTH * 3 + 1) * TB)
            act.dma_start(out.rearrange("(t p) d -> p t d", p=P), x[:]).then_inc(stored, 16)
            act.wait_ge(stored, 16)

        @block.vector
        def _(dve):
            st = Steps(dve, dve_step)

            def split_lo(slot, rslot, count, width=PW):
                dve.wait_ge(hi_ready, count)
                dve.tensor_tensor(w_lo[:, slot, 0:width], raw[:, rslot, 0:width],
                                  w_hi[:, slot, 0:width].bitcast(F32), ALU.subtract).then_inc(lo_ready, 1)

            dve.sem_inc(up_mul_ready, 1)
            for s in range(2):
                dve.sem_inc(acc_free[s], 1)
                dve.sem_inc(up_free[s], 1)
            for b in range(4):
                dve.sem_inc(bank_free[b], 1)
            dve.memset(o_r[:], 1.0)
            dve.wait_ge(first_here, 80)
            dve.tensor_copy(posk[:], posk_i[:])
            st.done(dve.tensor_copy(posq[:], posq_i[:]))
            dve.tensor_scalar(rel[:, 0:P], posk[:, 0:P], posq[:, 0:1], None, ALU.subtract)
            dve.tensor_scalar(rel[:, P:384], posk[:], posq[:, 1:2], None, ALU.subtract)
            dve.tensor_tensor(dtab[:, 0:15, :], tab[:, 0:15, :], tab[:, 1:16, :], ALU.subtract)
            dve.tensor_tensor(dtab[:, 15:16, :], tab[:, 17:18, :], tab[:, 0:1, :], ALU.subtract)
            st.done(dve.tensor_tensor(dtab[:, 16:30, :], tab[:, 18:32, :], tab[:, 17:31, :], ALU.subtract))
            dve.sem_inc(tab_ready, 1)
            for tb in range(TB):
                ins = dve.tensor_scalar(ang[:, tb, :], inv[:], posq[:, tb:tb + 1], None, ALU.mult)
            st.done(ins)
            inv2pi, magic = float(np.float32(0.5 / np.pi)), 12582912.0
            c1 = 6.28125
            c2 = float(np.float32(np.round((2 * np.pi - c1) * 2 ** 21) / 2 ** 21))
            c3 = float(np.float32(2 * np.pi - c1 - c2))
            for a, quarter in enumerate((0.25, 0.0)):
                t = trig[:, a]
                st.done(dve.tensor_scalar(t, ang[:], inv2pi, quarter, ALU.mult, ALU.add))
                st.done(dve.tensor_scalar(t, t, magic, None, ALU.add))
                st.done(dve.tensor_scalar(t, t, magic, None, ALU.subtract))
                r = kr[:, :, 0:HR]
                st.done(dve.scalar_tensor_tensor(r, t, -c1, ang[:], ALU.mult, ALU.add))
                st.done(dve.scalar_tensor_tensor(r, t, -c2, r, ALU.mult, ALU.add))
                st.done(dve.scalar_tensor_tensor(r, t, -c3, r, ALU.mult, ALU.add))
                st.done(dve.tensor_scalar(r, r, float(quarter * 2 * np.pi), None, ALU.add))
                st.done(dve.tensor_scalar(t, r, 3.1415925, -3.1415925, ALU.min, ALU.max))
            dve.sem_inc(setup_dve, 1)
            for p in range(SPL):
                split_lo(p, p, p + 1, piece_width(p))

            def newton(a, b):
                st.done(dve.tensor_tensor(rst[:, a:b], rs0[:, a:b], rs0[:, a:b], ALU.mult))
                st.done(dve.tensor_tensor(rst[:, a:b], rst[:, a:b], var[:, a:b], ALU.mult))
                st.done(dve.tensor_scalar(rst[:, a:b], rst[:, a:b], -0.5, 1.5, ALU.mult, ALU.add))
                st.done(dve.tensor_tensor(rst[:, a:b], rst[:, a:b], rs0[:, a:b], ALU.mult))

            dve.wait_ge(setup_act, 2)
            st.done(dve.tensor_scalar(var[:, 0:TB], ssq[:, 0:TB], 1.0 / D, EPS, ALU.mult, ALU.add))
            dve.sem_inc(setup_dve, 1)
            dve.wait_ge(setup_act, 3)
            newton(0, TB)
            dve.wait_ge(setup_pool, 1)
            for tb in range(TB):
                ins = dve.tensor_scalar(diag_m[:, tb, :], ident[:], rst[:, tb:tb + 1], None, ALU.mult)
            ins.then_inc(diagm_ready, 1)
            dve.wait_ge(diagm_ready, 1)
            dve.sem_inc(x_ready, TB)
            SET = st.n

            with dve.Fori(0, DEPTH) as l:
                st.base, st.n = l * DVE_STEPS + SET, 0

                def split(p):
                    split_lo(p % SPL, p % RAW, l * NPIECES + p + 1, piece_width(p % NPIECES))

                def split_dyn(p0, j, i, per):
                    q = p0 + j
                    split_lo(q % SPL, q % RAW, l * NPIECES + i * per + (q + 1))

                def read_bank(item):
                    dve.wait_ge(bank_done, l * NITEMS + ITEM[item] + 1)
                    return bank(item)

                def free_bank(ins, item):
                    ins.then_inc(bank_free[ITEM[item] % 4], 1)

                def tsplit(item):
                    dst, chunks, gains = tsplit_job(item)
                    b = bank(item)
                    dve.wait_ge(tsplit_hi, l * NTSPLIT + TSPLIT[item] + 1)
                    for kk, c in enumerate(chunks):
                        src, hi = b[:, kk * SEQ:(kk + 1) * SEQ], dst[:, c, 0, :].bitcast(F32)
                        if gains is None:
                            ins = dve.tensor_tensor(dst[:, c, 1, :], src, hi, ALU.subtract)
                        else:
                            ins = dve.scalar_tensor_tensor(dst[:, c, 1, :], src, cols[:, gains[kk]:gains[kk] + 1], hi,
                                                           ALU.mult, ALU.subtract)
                    free_bank(ins, item)

                def rstd(name, a, b, n, src=None):
                    src = ssq[:, a:b] if src is None else src
                    dve.tensor_scalar(var[:, a:b], src, 1.0 / n, EPS, ALU.mult, ALU.add).then_inc(var_ready, 1)
                    dve.wait_ge(rs0_ready, l * NRSTD + RSTD[name] + 1)
                    newton(a, b)

                def x_norm(k, name):
                    dve.wait_ge(ssq_ready, l * 7 + (2, 5, 7)[k])
                    rstd(name, 0, TB, D)
                    for tb in range(TB):
                        ins = dve.tensor_scalar(diag[:, tb, :], ident[:], rst[:, tb:tb + 1], None, ALU.mult)
                    ins.then_inc(diag_ready, 1)

                def t_evac(g, dst):
                    dve.wait_ge(t_lo_ready, l * len(T_GROUPS) + T_GROUPS.index(g) + 1)
                    dve.tensor_tensor(dst, ps[:, 2 * (g % 2):2 * (g % 2) + 2, 0:SEQ], t_lo[:], ALU.add).then_inc(
                        acc_free[g % 2], 1)

                def x_update(name, yt, k):
                    dve.wait_ge(y_gained, l * 12 + 4 * k + 4)
                    st.done(dve.tensor_reduce(ssq[:, 0:TB], ysq[:], AX, ALU.add))
                    rstd(name, 0, TB, D)
                    for tb in range(TB):
                        dve.scalar_tensor_tensor(x[:, tb, :], yt[:, tb, :], rst[:, tb:tb + 1], x[:, tb, :],
                                                 ALU.mult, ALU.add).then_inc(x_ready, 1)

                x_norm(0, "h1")
                dve.wait_ge(par_here, l * 32 + 32)
                lp = lam_prod.rearrange("p a h d -> p (a h d)")[:, 0:128].rearrange("p (m d) -> p m d", m=2)
                lrow = rows[:, RLAM:RLAM + 256].rearrange("p (m a d) -> p m a d", m=2, a=2)
                st.done(dve.tensor_tensor(lp, lrow[:, :, 0, :], lrow[:, :, 1, :], ALU.mult))
                dve.tensor_reduce(lamv[:, 0:2], lp, AX, ALU.add).then_inc(lam_prod_ready, 1)
                dve.wait_ge(lam_exp_ready, l + 1)
                st.done(dve.tensor_tensor(lamv[:, 4:5], lamv[:, 2:3], lamv[:, 3:4], ALU.subtract))
                st.done(dve.tensor_tensor(lamv[:, 4:5], lamv[:, 4:5], rows[:, RINIT:RINIT + 1], ALU.add))
                for i in range(8):
                    tsplit(("h1", i))

                for step in STEPS:
                    kind = step[0]
                    if kind == "split":
                        split(step[1])
                    elif kind == "evac":
                        gi = step[1]
                        name = W_IN_GROUPS[gi][0]
                        if W_IN_GROUPS[gi][1] == "T":
                            t, i = {"qa": qa_t, "ka": ka_t, "qb": qb_t, "kb": kb_t}[name[:2]], int(name[2])
                            t_evac(gi, t[:, 2 * i:2 * i + 2, :])
                        elif name == "cq":
                            pass
                    elif kind == "latent_stats":
                        dve.wait_ge(ssq_ready, l * 7 + 3)
                        dve.tensor_scalar(var[:, 0:2], ssq[:, 0:2], 1.0 / Q_LORA, EPS, ALU.mult, ALU.add)
                        dve.tensor_scalar(var[:, 2:4], ssq[:, 2:4], 1.0 / KV_LORA, EPS, ALU.mult, ALU.add).then_inc(var_ready, 1)
                        dve.wait_ge(rs0_ready, l * NRSTD + RSTD["latent"] + 1)
                        newton(0, 4)
                        dve.sem_inc(rst_ready, 1)
                        dve.wait_ge(*acc_read(l, GROUP["ckv"]))
                        dve.wait_ge(setup_act, 1)
                        k1, k2 = ckv[:, :, 256:256 + HR], ckv[:, :, 256 + HR:256 + 2 * HR]
                        ra, rb = rope_b[:, :, 0, :], rope_c[:, :, 0, :]
                        dve.tensor_tensor(kr[:, :, 0:HR], k1, trig[:, 0], ALU.mult)
                        dve.tensor_tensor(ra, k2, trig[:, 1], ALU.mult)
                        dve.tensor_tensor(kr[:, :, HR:], k2, trig[:, 0], ALU.mult)
                        st.done(dve.tensor_tensor(rb, k1, trig[:, 1], ALU.mult))
                        dve.tensor_tensor(kr[:, :, 0:HR], kr[:, :, 0:HR], ra, ALU.subtract)
                        st.done(dve.tensor_tensor(kr[:, :, HR:], kr[:, :, HR:], rb, ALU.add))
                    elif kind == "latent_T":
                        tsplit(step)
                    elif kind == "rope_q":
                        dve.wait_ge(*acc_read(l, GROUP["uqa"]))
                        dve.wait_ge(*acc_read(l, GROUP["small"]))
                        for tb in range(TB):
                            q1 = q_nat[:, tb, :, D_NOPE:D_NOPE + HR]
                            q2 = q_nat[:, tb, :, D_NOPE + HR:]
                            c = trig[:, 0, tb:tb + 1, :].to_broadcast([P, H_C, HR])
                            s = trig[:, 1, tb:tb + 1, :].to_broadcast([P, H_C, HR])
                            dve.tensor_tensor(rope_a[:, tb], q2, s, ALU.mult)
                            dve.tensor_tensor(rope_b[:, tb], q1, s, ALU.mult)
                            dve.tensor_tensor(rope_c[:, tb], q1, c, ALU.mult)
                            st.done(dve.tensor_tensor(q2, q2, c, ALU.mult))
                            dve.tensor_tensor(q1, rope_c[:, tb], rope_a[:, tb], ALU.subtract)
                            st.done(dve.tensor_tensor(q2, q2, rope_b[:, tb], ALU.add))
                    elif kind == "k_cat":
                        dve.wait_ge(*acc_read(l, GROUP["ukv1"]))
                        for tb in range(TB):
                            ins = dve.tensor_copy(k_cat[:, tb, :, D_NOPE:], kr[:, tb:tb + 1, :].to_broadcast([P, H_C, D_ROPE]))
                        ins.then_inc(k_cat_ready, 1)
                    elif kind == "forget":
                        dve.wait_ge(*acc_read(l, GROUP["vbf"]))
                        bf = rows[:, RBF:RBF + 2 * H_B].unsqueeze(1).to_broadcast([P, TB, 2 * H_B])
                        st.done(dve.tensor_tensor(z_f[:], z_f[:], bf, ALU.add))
                        dve.scalar_tensor_tensor(e_f[:], z_f[:], -1.0, z_f[:], ALU.mult, ALU.max).then_inc(f_abs, 1)
                        dve.wait_ge(f_exp, l + 1)
                        dve.tensor_scalar(e_f[:], e_f[:], 1.0, None, ALU.add).then_inc(f_one, 1)
                        st.done(dve.tensor_scalar(z_f[:], z_f[:], 0.0, None, ALU.min))
                        dve.wait_ge(f_ln, l + 1)
                        dve.tensor_tensor(z_f[:], z_f[:], e_f[:], ALU.subtract).then_inc(lf_ready, 1)
                    elif kind == "forget_scan":
                        n2 = 2 * H_B
                        b = read_bank(step)
                        st.done(dve.memset(lf_ones[0:n2, :], 1.0))
                        ins = dve.tensor_tensor_scan(f_row[0:n2, :], lf_ones[0:n2, :], b[0:n2, 0:SEQ], 0.0, ALU.mult, ALU.add)
                        free_bank(ins, step)
                        dve.wait_ge(*item_read(l, step))
                        st.done(dve.tensor_scalar(f_row[0:n2, :], f_row[0:n2, :], SQ_DB, None, ALU.mult))
                        st.done(dve.tensor_reduce(lamv[0:n2, 6:7], ident[0:n2, 0:H_B], AX, ALU.add))
                        st.done(dve.tensor_scalar(lamv[0:n2, 7:8], lamv[0:n2, 6:7], -1.0, 1.0, ALU.mult, ALU.add))
                        dve.tensor_scalar(fa[0:n2, :], f_row[0:n2, :], lamv[0:n2, 6:7], lamv[0:n2, 7:8], ALU.mult, ALU.add)
                        st.done(dve.tensor_scalar(f_row[0:n2, :], f_row[0:n2, :], -1.0, None, ALU.mult))
                        for h in range(H_B):
                            ins = dve.tensor_scalar(fb[0:n2, h, :], f_row[0:n2, :], ident[0:n2, H_B + h:H_B + h + 1],
                                                    ident[0:n2, h:h + 1], ALU.mult, ALU.add)
                        ins.then_inc(fab_ready, 1)
                    elif kind == "S":
                        n = step[1]
                        hk, h = HEAD_SEQ[n]
                        scale = {"A": DK_A, "B": D_B, "C": DQ_C}[hk] ** -0.5
                        if hk == "A":
                            dve.wait_ge(bias_done, 1)
                        else:
                            dve.wait_ge(setup_pool, 2)
                        tile = bias[:, h, :] if hk == "A" else (mask_b if hk == "B" else mask_c)[:]
                        for job in jobs_of(n):
                            j = JOB[job]
                            b = read_bank(("S", job))
                            if j >= 3:
                                prev = next(m for (m, mm_) in JOB if JOB[(m, mm_)] == j - 3)
                                dve.wait_ge(bank_done, l * NITEMS + ITEM[("T", prev)] + 1)
                            s = s_sb[:, j % 3, :]
                            ins = dve.scalar_tensor_tensor(s, b[:, 0:384], float(scale), tile, ALU.mult, ALU.add)
                            free_bank(ins, ("S", job))
                            dve.wait_ge(*item_read(l, ("S", job)))
                            dve.tensor_reduce(nmax[:, j % 4, 0:1], s[:, 0:P], AX, ALU.max, negate=True)
                            dve.tensor_reduce(nmax[:, j % 4, 1:2], s[:, P:384], AX, ALU.max, negate=True).then_inc(s_ready, 1)
                    elif kind == "N":
                        n = step[1]
                        hk, h = HEAD_SEQ[n]
                        jl = JOB[jobs_of(n)[-1]]
                        dve.wait_ge(p_ready, l * len(JOB) + jl + 1)
                        if hk == "A":
                            j0 = jl - 1
                            s0, s1 = s_sb[:, j0 % 3, :], s_sb[:, jl % 3, :]
                            dve.reciprocal(rcp[:, 0, :], sums[:, j0 % 4, :])
                            st.done(dve.reciprocal(rcp[:, 1, :], sums[:, jl % 4, :]))
                            st.done(dve.tensor_scalar(rcp[:, 1, :], rcp[:, 1, :], lamv[:, 4:5], None, ALU.mult))
                            for tb, (o, nk) in enumerate(((0, P), (P, SEQ))):
                                ins = dve.tensor_scalar(s1[:, o:o + nk], s1[:, o:o + nk], rcp[:, 1, tb:tb + 1], None, ALU.mult)
                            st.done(ins)
                            for tb, (o, nk) in enumerate(((0, P), (P, SEQ))):
                                ins = dve.scalar_tensor_tensor(s0[:, o:o + nk], s0[:, o:o + nk], rcp[:, 0, tb:tb + 1],
                                                               s1[:, o:o + nk], ALU.mult, ALU.subtract)
                            ins.then_inc(pn_ready, 1)
                        else:
                            col = (H_A if hk == "B" else H_A + H_B) + h
                            st.done(dve.reciprocal(o_r[:, :, col], sums[:, jl % 4, :]))
                    elif kind == "O":
                        n = step[1]
                        hk, h = HEAD_SEQ[n]
                        col = {"A": 0, "B": H_A, "C": H_A + H_B}[hk] + h
                        b = read_bank(step)
                        ins = dve.tensor_copy(o_nat[:, :, col * P:(col + 1) * P], b[:, 0:2 * P].rearrange("p (t d) -> p t d", t=TB))
                        free_bank(ins, step)
                    elif kind == "onorm":
                        h0, h1 = step[1:]
                        nh = h1 - h0
                        k = {10: 0, 0: 1, 4: 2}[h0]
                        dve.wait_ge(osq_ready, l * 3 + k + 1)
                        sq = sq_tile(h0, h1)
                        v = o_sq[:, :, h0:h1]
                        r = o_r[:, :, h0:h1]
                        st.done(dve.tensor_reduce(v, sq, AX, ALU.add))
                        st.done(dve.tensor_tensor(v, v, r, ALU.mult))
                        flat = ssq[:, 0:TB * nh].rearrange("p (t h) -> p t h", t=TB)
                        st.done(dve.tensor_tensor(flat, v, r, ALU.mult))
                        rstd(f"o{h0}", 0, TB * nh, P)
                        ins = dve.tensor_tensor(v, rst[:, 0:TB * nh].rearrange("p (t h) -> p t h", t=TB), r, ALU.mult)
                        st.done(ins)
                        if h0 == 0:
                            st.done(dve.tensor_scalar(v, v, rows[:, RINIT + 1:RINIT + 2], None, ALU.mult))
                        dve.sem_inc(oscl_ready, 1)
                    elif kind == "head_T":
                        tsplit(step)

                with dve.Fori(0, 2) as i:
                    for k in range(2):
                        for j in range(8):
                            split_dyn(P_OUT + 8 * k + SPL, j, i, 16)
                for i in range(8):
                    tsplit(("mem_T", i))
                x_update("y1", y_a, 0)
                x_norm(1, "h2")
                for k in range(2):
                    for j in range(4):
                        split(P_MEMK + 4 * k + SPL + j)
                    t_evac(G_MEMK + k, kx_t[:, 2 * k:2 * k + 2, :])
                for i in range(8):
                    tsplit(("h2", i))
                for k in range(2):
                    for j in range(4):
                        split(P_WQ + 4 * k + SPL + j)
                    t_evac(G_WQ + k, qx_t[:, 2 * k:2 * k + 2, :])
                for h in range(H_X):
                    b = read_bank(("XS", h))
                    st.done(dve.tensor_reduce(nmax[:, h, :], b.rearrange("p (t k) -> p t k", t=TB), AX, ALU.max, negate=True))
                    dve.tensor_scalar(nmax[:, h, :], nmax[:, h, :], float(D_X ** -0.5), None, ALU.mult).then_inc(xm_ready, 1)
                for j in range(8):
                    split(P_MEMV + SPL + j)
                    if j < H_X:
                        h = j
                        dve.wait_ge(*item_read(l, ("XS", h)))
                        st.done(dve.reciprocal(rcp[:, h, :], sums[:, h, :]))
                        for tb in range(TB):
                            t = (px if h < 2 else px2)[:, h % 2, tb, :]
                            ins = dve.tensor_scalar(t, t, rcp[:, h, tb:tb + 1], None, ALU.mult)
                        ins.then_inc(xpn_ready, 1)
                for h in range(H_X):
                    tsplit(("XO", h))
                for j in range(8):
                    split(P_WO + SPL + j)
                x_update("y2", y_a, 1)
                x_norm(2, "h3")
                for i in range(8):
                    tsplit(("h3", i))

                def up_split(i, half, j):
                    split_dyn(P_UP + 8 * half + SPL, j, i, 16)

                def up_tail(i, half, j):
                    g = i * 2 + half
                    if j == 0:
                        dve.wait_ge(up_lo_ready, l * UPG + g + 1)
                        dve.tensor_tensor(up_u[:], ps[:, 4 * half:4 * half + 4, 0:SEQ], up_lo[:], ALU.add).then_inc(up_free[half], 1)
                    if j == 2:
                        dve.wait_ge(up_aff_ready, l * UPG + g + 1)
                        for nt in range(4):
                            ins = dve.scalar_tensor_tensor(up_c[:, nt, 1:SEQ], up_u[:, nt, 0:SEQ - 1], cw[:, 4 * nt + 1:4 * nt + 2],
                                                           up_c[:, nt, 1:SEQ], ALU.mult, ALU.add)
                        ins.then_inc(up_tap, 1)
                        dve.wait_ge(up_tap, l * UPG + g + 1)
                        for nt in range(4):
                            ins = dve.scalar_tensor_tensor(up_c[:, nt, 2:SEQ], up_u[:, nt, 0:SEQ - 2], cw[:, 4 * nt:4 * nt + 1],
                                                           up_c[:, nt, 2:SEQ], ALU.mult, ALU.add)
                        ins.then_inc(up_conv_ready, 1)
                    if j == 4:
                        dve.wait_ge(up_gelu_ready, l * UPG + g + 1)
                        dve.tensor_tensor(up_a[:], up_g[:], up_c[:, 2:4, :], ALU.mult).then_inc(up_mul_ready, 1)
                    if j == 6:
                        dve.wait_ge(up_hi_ready, l * UPG + g + 1)
                        dve.tensor_tensor(act_t[:, bass.ds(2 * g, 2), 1, :], up_a[:],
                                          act_t[:, bass.ds(2 * g, 2), 0, :].bitcast(F32), ALU.subtract).then_inc(act_ready, 1)

                for j in range(8):
                    up_split(0, 0, j)
                with dve.Fori(0, UPG // 2 - 1) as i:
                    for j in range(8):
                        up_split(i, 1, j)
                        up_tail(i, 0, j)
                    for j in range(8):
                        split_dyn(P_UP + 16 + SPL, j, i, 16)
                        up_tail(i, 1, j)
                for j in range(8):
                    up_split(UPG // 2 - 1, 1, j)
                    up_tail(UPG // 2 - 1, 0, j)
                for j in range(8):
                    split(P_DOWN + SPL + j)
                    up_tail(UPG // 2 - 1, 1, j)
                for j in range(8, 64):
                    split(P_DOWN + SPL + j)
                x_update("y3", y_f, 2)
                assert st.n == DVE_STEPS, ("DVE_STEPS", st.n)

        @block.gpsimd
        def _(pool):
            pool.memset(ident[:], 0.0)
            pool.memset(mask_b[:], 0.0)
            pool.memset(mask_c[:], 0.0).then_inc(pool_step, 1)
            pool.wait_ge(pool_step, 1)
            pool.affine_select(out=ident[:], in_=ident[:], compare_op=ALU.not_equal, fill=1.0, base=0,
                               pattern=[[-1, P]], channel_multiplier=1).then_inc(setup_pool, 1)
            pool.affine_select(out=mask_b[:, 0:P], in_=mask_b[:, 0:P], compare_op=ALU.is_ge, fill=NEG, base=0,
                               pattern=[[-1, P]], channel_multiplier=1).then_inc(pool_step, 1)
            pool.affine_select(out=mask_b[:, P:384], in_=mask_b[:, P:384], compare_op=ALU.is_ge, fill=NEG, base=P,
                               pattern=[[-1, SEQ]], channel_multiplier=1).then_inc(pool_step, 1)
            pool.memset(mask_c[0:CHUNK, CHUNK:P], NEG).then_inc(pool_step, 1)
            pool.memset(mask_c[0:CHUNK, 384 - CHUNK:384], NEG).then_inc(pool_step, 1)
            pool.wait_ge(pool_step, 5)
            pool.sem_inc(setup_pool, 1)
            pool.wait_ge(tab_ready, 1)
            for h in range(H_A):
                ins = pool.tensor_scalar(bias[:, h, :], mask_c[:], tab[:, 15, h:h + 1], 0.0, ALU.add, ALU.add)
            ins.then_inc(pool_step, 1)
            n = 6
            pool.wait_ge(pool_step, n)
            edges = [(-t + 1, j) for j, t in enumerate(NEAR)] + [(t, 15 + j) for j, t in enumerate(NEAR)]
            for edge, j in edges:
                pool.tensor_scalar(ind[:], rel[:], float(edge), 1.0, ALU.is_ge, ALU.mult).then_inc(pool_step, 1)
                n += 1
                pool.wait_ge(pool_step, n)
                pool.tensor_tensor(btmp[:], ind[:].unsqueeze(1).to_broadcast([P, H_A, 384]),
                                   dtab[:, j, :].unsqueeze(2).to_broadcast([P, H_A, 384]), ALU.mult).then_inc(pool_step, 1)
                n += 1
                pool.wait_ge(pool_step, n)
                pool.tensor_tensor(bias[:], bias[:], btmp[:], ALU.add).then_inc(pool_step, 1)
                n += 1
                pool.wait_ge(pool_step, n)
            pool.sem_inc(bias_done, 1)

            with pool.Fori(0, DEPTH) as l:
                for step in STEPS:
                    if step[0] != "onorm":
                        continue
                    h0, h1 = step[1:]
                    k = {10: 0, 0: 1, 4: 2}[h0]
                    pool.wait_ge(*item_read(l, ("O", {10: 5, 0: 9, 4: 15}[h0])))
                    src = o_nat[:, :, h0 * P:h1 * P].rearrange("p t (h d) -> p t h d", d=P)
                    sq = sq_tile(h0, h1)
                    for tb in range(TB):
                        ins = pool.tensor_tensor(sq[:, tb], src[:, tb], src[:, tb], ALU.mult)
                    ins.then_inc(osq_ready, 1)
                    pool.wait_ge(oscl_ready, l * 3 + k + 1)
                    for tb in range(TB):
                        ins = pool.tensor_tensor(src[:, tb], src[:, tb],
                                                 o_sq[:, tb, h0:h1].unsqueeze(2).to_broadcast([P, h1 - h0, P]), ALU.mult)
                    ins.then_inc(on_ready, 1)

                def gains(yt, gt, k, o, dyn=0):
                    pool.wait_ge(gain_here, l * 48 + 16 * (k + 1))
                    pool.wait_ge(y_sq, l * 12 + dyn + (4 * k + 1))
                    for tb in range(TB):
                        ins = pool.tensor_tensor(yt[:, tb, bass.ds(o, 512)], yt[:, tb, bass.ds(o, 512)],
                                                 gt[:, bass.ds(o, 512)], ALU.mult)
                    ins.then_inc(y_gained, 1)

                with pool.Fori(0, 4) as i:
                    gains(y_a, gain_a, 0, i * 512, i)
                with pool.Fori(0, 4) as i:
                    gains(y_a, gain_a, 1, i * 512, i)
                with pool.Fori(0, UPG // 2) as i:
                    for half in range(2):
                        g = i * 2 + half
                        pool.wait_ge(up_mul_ready, l * UPG + g + 1)
                        pool.tensor_copy(cw[:], cols[:, bass.ds(g * 16 + CCONV, 16)]).then_inc(cw_ready, 1)
                        pool.wait_ge(cw_ready, l * UPG + g + 1)
                        pool.wait_ge(up_free[half], l * (UPG // 2) + i + 2)
                        pool.sem_inc(gate, 1)
                        for nt in range(4):
                            ins = pool.tensor_scalar(up_c[:, nt, :], up_u[:, nt, :], cw[:, 4 * nt + 2:4 * nt + 3],
                                                     cw[:, 4 * nt + 3:4 * nt + 4], ALU.mult, ALU.add)
                        ins.then_inc(up_aff_ready, 1)
                with pool.Fori(0, 4) as i:
                    gains(y_f, gain_f, 2, i * 512, i)


def _stream(w):
    def piece(rows_cols, chunks):
        n = rows_cols.shape[1]
        a = rows_cols.reshape(chunks, P, n).transpose(1, 0, 2).reshape(P, chunks * n)
        if a.shape[1] < PW:
            a = np.concatenate([a, np.zeros((P, PW - a.shape[1]), a.dtype)], axis=1)
        return a

    out = np.zeros((DEPTH * NPIECES + SPL, P, PW), np.float32)
    n = 0

    def put(mat, chunks):
        nonlocal n
        rows_ = chunks * P
        for k in range(mat.shape[0] // rows_):
            out[n] = piece(mat[k * rows_:(k + 1) * rows_], chunks)
            n += 1

    for l in range(DEPTH):
        w_in, uq, ukv = w["w_in"][l], w["w_uq"][l], w["w_ukv"][l]
        f = w_in[:, C_F:C_F + H_B]
        cols_ = {"cq": w_in[:, C_CQ:C_CQ + Q_LORA], "ckv": w_in[:, C_CKV:C_CKV + KV_LORA + D_ROPE],
                 "va": w_in[:, C_VA:C_VA + 512], "vb": w_in[:, C_VB:C_VB + 512],
                 "vbf": np.concatenate([w_in[:, C_VB + 512:C_VB + 768], f, f], axis=1)}
        for name, kind, _, chunks, _ in W_IN_GROUPS:
            if kind == "T":
                c0 = {"qa": C_QA, "ka": C_KA, "qb": C_QB, "kb": C_KB}[name[:2]] + 256 * int(name[2])
                put(w_in[:, c0:c0 + 256], chunks)
            elif name == "uqa":
                put(uq[:, 0:512], 2)
            elif name == "small":
                put(uq[:, 512:576], 2)
                put(ukv[:, 1024:1152], 1)
            elif name in ("ukv0", "ukv1"):
                put(ukv[:, 512 * int(name[3]):512 * int(name[3]) + 512], 2)
            else:
                put(cols_[name], chunks)
        w_out = w["w_out"][l].reshape(KC, P, D)[HEAD_ORDER].reshape(D, D)
        for k in range(4):
            put(w_out[:, 512 * k:512 * k + 512], 2)
        for k in range(2):
            put(w["wkv_x"][l][:, 256 * k:256 * k + 256], 4)
        for k in range(2):
            put(w["wq_x"][l][:, 256 * k:256 * k + 256], 4)
        put(w["wkv_x"][l][:, 512:1024], 2)
        for k in range(4):
            put(w["wo_x"][l][:, 512 * k:512 * k + 512], 2)
        up = w["w_up"][l].reshape(D, 2, UPG, 256)
        for g in range(UPG):
            put(up[:, :, g].reshape(D, 512), 2)
        for k in range(4):
            put(w["w_down"][l][:, 512 * k:512 * k + 512], 2)
    assert n == DEPTH * NPIECES
    return out


def kernel(**inputs):
    import concourse.bacc as bacc
    from concourse.bass_utils import run_bass_kernel_spmd

    w = {k: np.ascontiguousarray(v) for k, v in inputs.items()}
    cols = np.zeros((DEPTH, P, NCOL), np.float32)
    rows = np.zeros((DEPTH, NROW), np.float32)
    gains = np.zeros((DEPTH * 3, D), np.float32)
    for l in range(DEPTH):
        def column(v):
            return v.reshape(-1, P).T
        g = w["norm_gains"][l]
        cols[l, :, CG0:CG0 + KC] = column(g[0])
        cols[l, :, CG2:CG2 + KC] = column(g[2])
        cols[l, :, CG4:CG4 + KC] = column(g[4])
        cols[l, :, CMEM:CMEM + KC] = column(w["mem_norm"][l])
        cols[l, :, CHEAD:CHEAD + KC] = column(w["head_norm"][l])
        cols[l, :, CQN:CQN + 4] = column(w["q_norm"][l])
        cols[l, :, CKVN:CKVN + 2] = column(w["kv_norm"][l])
        conv = np.concatenate([w["conv_w"][l], w["conv_b"][l][None]], axis=0)
        conv = conv.reshape(4, 2, UPG, 2, P).transpose(4, 2, 1, 3, 0)
        cols[l, :, CCONV:] = conv.reshape(P, UPG * 16)
        rows[l, RLAM:RLAM + 256] = w["lam"][l].reshape(-1)
        rows[l, RBF:RBF + H_B] = w["b_forget"][l]
        rows[l, RBF + H_B:RBF + 2 * H_B] = w["b_forget"][l]
        init = 0.8 - 0.6 * np.exp(-0.3 * l)
        rows[l, RINIT], rows[l, RINIT + 1] = init, 1.0 - init
        gains[3 * l:3 * l + 3] = g[1::2]
    inv = (10000.0 ** (-np.arange(0, D_ROPE, 2, dtype=np.float64) / D_ROPE)).astype(np.float32)
    arrays = {"stream": _stream(w), "x_in": w["x"].reshape(SEQ, D), "mem_in": w["mem"].reshape(SEQ, D),
              "pos_in": w["positions"].reshape(SEQ), "posq_in": w["positions"].reshape(TB, P).T, "rel_in": w["rel_bias"], "cols_in": cols, "rows_in": rows,
              "gains_in": gains, "inv_in": inv}
    arrays = {k: np.ascontiguousarray(a) for k, a in arrays.items()}
    nc = bacc.Bacc("TRN2", target_bir_lowering=False, num_devices=1)
    args = [nc.dram_tensor(n, a.shape, mybir.dt.from_np(a.dtype), kind="ExternalInput").ap() for n, a in arrays.items()]
    out = nc.dram_tensor("out", (SEQ, D), F32, kind="ExternalOutput").ap()
    build(nc, *args, out)
    r = run_bass_kernel_spmd(nc, [arrays], core_ids=[0])
    return r.results[0]["out"].reshape(1, SEQ, D)
```

```python
from contextlib import ExitStack

import numpy as np
import concourse.bass as bass
from concourse import mybir

F32 = mybir.dt.float32
F32R = mybir.dt.float32r
BF16 = mybir.dt.bfloat16
I32 = mybir.dt.int32
ALU = mybir.AluOpType
ACT = mybir.ActivationFunctionType
AX = mybir.AxisListType.X

P = 128
D, SEQ, DEPTH = 2048, 256, 2
TB = SEQ // P
KC = D // P
H_A, DK_A, H_B, D_B, H_C = 4, 64, 6, 128, 6
Q_LORA, KV_LORA, D_NOPE, D_ROPE = 512, 256, 64, 32
D_FF, H_X, D_X, CHUNK = 4096, 4, 128, 64
DQ_C = D_NOPE + D_ROPE
EPS, NEG = 1e-6, -1e30
HEADS = H_A + H_B + H_C
HR = D_ROPE // 2
C_QA, C_KA, C_VA, C_QB, C_KB, C_VB = 0, 512, 1024, 1536, 2304, 3072
C_F, C_CQ, C_CKV = 3840, 3846, 4358

PW = 1024
RAW = 8
SPL = 4

W_IN_GROUPS = [
    ("cq", "nat", 8, 2, 512), ("ckv", "nat", 8, 2, KV_LORA + D_ROPE),
    ("vbf", "nat", 8, 2, 256 + 2 * H_B), ("vb", "nat", 8, 2, 512),
    ("uqa", "nat", 2, 2, 512), ("small", "nat", 4, 0, 0), ("ukv0", "nat", 1, 2, 512), ("ukv1", "nat", 1, 2, 512),
    ("va", "nat", 8, 2, 512),
    ("qb0", "T", 4, 4, 256), ("kb0", "T", 4, 4, 256), ("qb1", "T", 4, 4, 256), ("kb1", "T", 4, 4, 256),
    ("qb2", "T", 4, 4, 256), ("kb2", "T", 4, 4, 256),
    ("qa0", "T", 4, 4, 256), ("ka0", "T", 4, 4, 256), ("qa1", "T", 4, 4, 256), ("ka1", "T", 4, 4, 256),
]
N_IN = sum(g[2] for g in W_IN_GROUPS)
P_OUT = N_IN
P_MEMK = P_OUT + 32
P_WQ = P_MEMK + 8
P_MEMV = P_WQ + 8
P_WO = P_MEMV + 8
P_UP = P_WO + 8
UPG = 16
P_DOWN = P_UP + 8 * UPG
NPIECES = P_DOWN + 64
assert NPIECES % RAW == 0 and all(p % RAW == 0 for p in (P_OUT, P_MEMK, P_WQ, P_MEMV, P_WO, P_UP, P_DOWN))
G_OUT = len(W_IN_GROUPS)
G_MEMK, G_WQ, G_MEMV, G_WO, G_DOWN, NGROUPS = G_OUT + 4, G_OUT + 6, G_OUT + 8, G_OUT + 9, G_OUT + 13, G_OUT + 17
assert NGROUPS % 2 == 0

HEAD_ORDER = [10, 11, 12, 13, 14, 15, 4, 5, 6, 7, 8, 9, 0, 1, 2, 3]
OUT_HEAD = 6
OUT_ORDER = ([(0, j) for j in range(OUT_HEAD)] + [(1, j) for j in range(OUT_HEAD)]
             + [(0, j) for j in range(OUT_HEAD, 8)] + [(1, j) for j in range(OUT_HEAD, 8)]
             + [(k, j) for k in (2, 3) for j in range(8)])

CG2, CG4, CMEM, CHEAD, CQN, CKVN, CCONV = 0, 16, 32, 48, 64, 68, 70
NCOL = CCONV + 16 * UPG
RBF, RINIT = 0, 2 * H_B
NROW = RINIT + 2

NEAR = [1, 2, 3, 4, 5, 6, 7, 8, 14, 23, 39, 64, 108, 182, 305]
EDGES = [-t + 1 for t in NEAR] + NEAR
RSQRT_BITS = float(0x5f3759df)
SQ_DB = float(np.float32(np.sqrt(D_B)))

HEAD_SEQ = [("C", h) for h in range(H_C)] + [("B", h) for h in range(H_B)] + [("A", h) for h in range(H_A)]


def jobs_of(n):
    return [(n, m) for m in range(2 if HEAD_SEQ[n][0] == "A" else 1)]


JOB = {}
for _n in range(HEADS):
    for _j in jobs_of(_n):
        JOB[_j] = len(JOB)


BATCHES = {H_A + H_B: (HEADS, H_C - 1), H_A: (H_A + H_B, H_C + H_B - 1), 0: (H_A, HEADS - 1)}


def layer_steps():
    after = {}

    def at(p, *steps):
        after.setdefault(p, []).extend(steps)

    ends = {}
    p = 0
    for gi, (name, _, n, _, _) in enumerate(W_IN_GROUPS):
        p += n
        ends[name] = p - 1
        at(p - 1, ("evac", gi))
    for i in range(4, 8):
        at(i - 4, ("h1", i))
    at(3, ("x_stats", 0, 0))
    at(4, ("x_stats", 0, 1))
    at(5, ("x_rstd", 0))
    at(8, ("lam",))
    at(9, ("R", "h1"))
    for i, part in ((0, "squares"), (2, "rstd"), (4, "scale"), (5, "rope_k")):
        at(ends["ckv"] + i, ("latent", part))
    at(23, *[("latent_T", i) for i in range(2)])
    at(24, *[("latent_T", i) for i in range(2, 5)])
    for i, part in enumerate(("abs", "exp", "one", "ln", "log_f")):
        at(ends["vbf"] + 1 + i, ("forget", part))
    at(ends["vbf"] + 7, ("forget_scan",))
    at(ends["small"], ("rope_q",))
    at(ends["ukv1"], ("k_cat",))
    for h in range(6):
        at(ends["ukv1"] + 3 + h // 2, ("latent_qk_T", h))
    s_at = [44, 46, 48, 50, 52, 54, 57, 59, 65, 67, 73, 75, 83, 85, 89, 91]
    t_at = [46, 48, 50, 52, 54, 57, 59, 61, 67, 69, 75, 77, 86, 88, 92, 94]
    o_at = [48, 50, 52, 54, 57, 59, 61, 63, 69, 71, 77, 79, 88, 90, 94, 96]
    for q in range(P_OUT + 12):
        for n in range(HEADS):
            if o_at[n] == q:
                at(q, ("O", n))
            if o_at[n] + 1 == q:
                at(q, ("osq", n))
            if t_at[n] == q:
                at(q, ("T", n))
        for n in range(HEADS):
            if s_at[n] == q:
                at(q, ("S", n))
            if s_at[n] + 1 == q:
                at(q, ("N", n))
    at(61, ("onorm", 10))
    for i in range(3):
        at(63 + i, ("head_T", i))
    at(80, ("onorm", 4))
    for i in range(3, 6):
        at(79 + i, ("head_T", i))
    at(97, ("load_gain", 0), ("onorm", 0))
    at(99, ("head_T", 6), ("head_T", 7))
    at(99, ("load_mem",))
    at(P_OUT + 13, ("evac", G_OUT))
    at(P_OUT + 15, ("evac", G_OUT + 1))
    for i in range(8):
        at(P_OUT + 18 + i, ("mem_T", i))
    at(P_OUT + 16, ("mem_stats", 0))
    at(P_OUT + 18, ("mem_stats", 1))
    at(P_OUT + 20, ("mem_rstd",))
    at(P_OUT + 22, ("R", "mem"))
    at(P_OUT + 23, ("evac", G_OUT + 2))
    at(P_OUT + 31, ("evac", G_OUT + 3), ("y_rstd", 0))
    at(P_MEMK + 3, ("evac", G_MEMK))
    at(P_MEMK + 7, ("evac", G_MEMK + 1))
    for i in range(8):
        at(P_MEMK + i // 2, ("upd", 0, i))
        at(P_MEMK + 3 + i // 2, ("h2", i))
    at(P_MEMK + 2, ("load_gain", 1), ("x_stats", 1, 0))
    at(P_MEMK + 4, ("x_stats", 1, 1))
    at(P_MEMK + 6, ("x_rstd", 1))
    at(P_WQ + 1, ("R", "h2"))
    at(P_WQ + 3, ("evac", G_WQ))
    at(P_WQ + 7, ("evac", G_WQ + 1))
    for h in range(H_X):
        at(P_MEMV + (0 if h < 2 else 1), ("XS", h))
        at(P_MEMV + 1 + h, ("XN", h))
        at(P_MEMV + 3 + h, ("XT", h))
    at(P_MEMV + 7, ("evac", G_MEMV), *[("XO", h) for h in range(H_X)])
    for k in range(4):
        at(P_WO + 2 * k + 1, ("evac", G_WO + k))
    at(P_WO + 7, ("y_rstd", 1))
    steps = []
    for p in range(P_UP):
        steps.append(("mm", p))
        steps.extend(sorted(after.get(p, []), key=lambda s: s[0] != "evac"))
        if p < P_UP - 1:
            steps.append(("split", p + SPL))
    steps += [("upd", 1, 0), ("upd", 1, 1), ("h3", 0), ("split", P_UP - 1 + SPL), ("upd", 1, 2)]
    for i in range(8):
        if i + 3 < 8:
            steps.append(("upd", 1, i + 3))
        if i in (2, 5):
            steps.append(("x_stats", 2, i // 5))
        if i < 7:
            steps.append(("h3", i + 1))
        if i == 6:
            steps.append(("x_rstd", 2))
        if i > 0:
            steps.append(("split", P_UP + i - 1 + SPL))
        steps.append(("mm", P_UP + i))
    steps += [("R", "h3"), ("split", P_UP + 7 + SPL)]
    return steps


H1_BEFORE = 4
END_STEPS = ([("upd", 2, i) for i in range(6)] + [("h1", 0), ("upd", 2, 6), ("upd", 2, 7)]
             + [("h1", i) for i in range(1, H1_BEFORE)])

STEPS = layer_steps()


def piece_group(p):
    for gi, (_, _, n, _, _) in enumerate(W_IN_GROUPS):
        if p < n:
            return gi, p
        p -= n


def piece_width(p):
    if p >= N_IN:
        return PW
    gi, j = piece_group(p)
    _, kind, _, ch, w = W_IN_GROUPS[gi]
    return P if ch == 0 else ch * w


def bank_items():
    items = []
    for s in STEPS + END_STEPS:
        if s[0] in ("latent_T", "latent_qk_T", "head_T", "O", "T", "forget_scan", "R", "mem_T", "h1", "h2", "h3",
                    "XS", "XT", "XO"):
            items.append(s)
        elif s[0] == "S":
            items += [("S", j) for j in jobs_of(s[1])]
    assert len(items) % 4 == 0, len(items)
    return items


ITEMS = bank_items()
ITEM = {name: w for w, name in enumerate(ITEMS)}
assert len(ITEM) == len(ITEMS)
NITEMS = len(ITEMS)

GROUP = {g[0]: i for i, g in enumerate(W_IN_GROUPS)}
GROUP_END = {}
_p = 0
for _i, _g in enumerate(W_IN_GROUPS):
    _p += _g[2]
    GROUP_END[_i] = _p
for _i in range(4):
    GROUP_END[G_OUT + _i] = P_OUT + OUT_ORDER.index((_i, 7)) + 1
    GROUP_END[G_WO + _i] = P_WO + 2 * (_i + 1)
    GROUP_END[G_DOWN + _i] = P_DOWN + 16 * (_i + 1)
for _i in range(2):
    GROUP_END[G_MEMK + _i] = P_MEMK + 4 * (_i + 1)
    GROUP_END[G_WQ + _i] = P_WQ + 4 * (_i + 1)
GROUP_END[G_MEMV] = P_MEMV + 8
T_GROUPS = [i for i, g in enumerate(W_IN_GROUPS) if g[1] == "T"] + [G_MEMK, G_MEMK + 1, G_WQ, G_WQ + 1]
T_BEFORE = dict(zip(T_GROUPS, [None] + T_GROUPS))

LATENT_CHUNKS = [[0, 1], [2], [3], [4], [5]]
TSPLITS = [s for s in STEPS + END_STEPS if s[0] in ("latent_T", "head_T", "mem_T", "h1", "h2", "h3", "XO")]
TSPLIT = {name: n for n, name in enumerate(TSPLITS)}
NTSPLIT = len(TSPLITS)

DVE_STEPS = 186


class Steps:

    def __init__(self, eng, sem):
        self.eng, self.sem, self.base, self.n = eng, sem, 0, 0

    def done(self, ins):
        ins.then_inc(self.sem, 1)
        self.n += 1
        self.eng.wait_ge(self.sem, self.base + self.n)


def build(nc, stream, x_in, mem_in, pos_in, posq_in, first_row_in, cols_in, h1_gains_in, rows_in, lam_in, gains_in, out):
    with ExitStack() as ctx:
        def sem(name):
            return ctx.enter_context(nc.semaphore(name))

        base = (nc.sbuf_base + 31) // 32 * 32
        K = 1024

        def sb(name, shape, off, dt=F32):
            n = int(np.prod(shape[1:])) * (2 if dt == BF16 else 4)
            assert base + off + n <= nc.sbuf_usable_end, (name, off, n)
            return nc.alloc_sbuf_tensor_at(name, shape, dt, offset=base + off)

        raw = sb("raw", [P, RAW, PW], 0)
        w_hi = sb("w_hi", [P, SPL, PW], 32 * K, F32R)
        w_lo = sb("w_lo", [P, SPL, PW], 48 * K, F32R)
        x = sb("x", [P, TB, D], 64 * K)
        h_t = sb("h_t", [P, KC, 2, SEQ], 80 * K, F32R)
        m_t = sb("m_t", [P, KC, 2, SEQ], 80 * K, F32R)
        BIG = 112 * K
        qa_t = sb("qa_t", [P, 4, SEQ], BIG)
        ka_t = sb("ka_t", [P, 4, SEQ], BIG + 4 * K)
        qb_t = sb("qb_t", [P, 6, SEQ], BIG + 8 * K)
        kb_t = sb("kb_t", [P, 6, SEQ], BIG + 14 * K)
        qc_t = sb("qc_t", [P, 6, SEQ], BIG + 20 * K)
        kc_t = sb("kc_t", [P, 6, SEQ], BIG + 26 * K)
        va = sb("va", [P, TB, 512], BIG + 32 * K)
        vb = sb("vb", [P, TB, 768], BIG + 36 * K)
        vc = sb("vc", [P, TB, 768], BIG + 42 * K)
        o_nat = sb("o_nat", [P, TB, D], BIG + 48 * K)
        o_t = sb("o_t", [P, HEADS, 2, SEQ], BIG, F32R)
        cq = sb("cq", [P, TB, Q_LORA], BIG + 8 * K)
        ckv = sb("ckv", [P, TB, KV_LORA + D_ROPE], BIG + 12 * K)
        q_nat = sb("q_nat", [P, TB, H_C, DQ_C], BIG + 8 * K)
        k_cat = sb("k_cat", [P, TB, H_C, DQ_C], BIG + 12 * K + 768)
        rope_a = sb("rope_a", [P, TB, H_C, HR], BIG + 17 * K + 512)
        rope_b = sb("rope_b", [P, TB, H_C, HR], BIG + 18 * K + 256)
        rope_c = sb("rope_c", [P, TB, H_C, HR], BIG + 19 * K)
        c_t = sb("c_t", [P, 6, 2, SEQ], BIG + 48 * K, F32R)
        lf_ones = sb("lf_ones", [P, SEQ], BIG + 15 * K)
        f_row = sb("f_row", [P, SEQ], BIG + 16 * K)
        rel = sb("rel", [P, 384], BIG)
        btmp = sb("btmp", [P, H_A, 384], BIG + 3 * K // 2)
        dtab = sb("dtab", [P, 30, H_A], BIG + 15 * K // 2)
        first_row = sb("first_row", [P, HR + 32 * H_A], BIG + 20 * K)
        inv, tab = first_row[:, 0:HR], first_row[:, HR:].rearrange("p (b h) -> p b h", h=H_A)
        posk_i = sb("posk_i", [P, SEQ], BIG + 21 * K, I32)
        posk = sb("posk", [P, SEQ], BIG + 22 * K)
        h2_t = sb("h2_t", [P, KC, 2, SEQ], BIG, F32R)
        y_a = sb("y_a", [P, 8, TB, 256], BIG + 32 * K)
        m_nat = sb("m_nat", [P, TB, D], BIG + 48 * K)
        kx_t = sb("kx_t", [P, H_X, SEQ], BIG + 48 * K)
        qx_t = sb("qx_t", [P, H_X, SEQ], BIG + 52 * K)
        vx = sb("vx", [P, TB, 512], BIG + 56 * K)
        px_t = sb("px_t", [P, H_X, 2, SEQ], BIG + 32 * K)
        px = sb("px", [P, H_X, TB, SEQ], BIG + 40 * K)
        xo_t = sb("xo_t", [P, 4, 2, SEQ], BIG, F32R)
        act_t = sb("act_t", [P, 2 * KC, 2, SEQ], BIG, F32R)
        gain_f = sb("gain_f", [P, D], 80 * K)
        y_f = sb("y_f", [P, 8, TB, 256], 96 * K)
        SCR = 176 * K
        s_sb = sb("s_sb", [P, 3, 384], SCR)
        p_t = sb("p_t", [P, 384], SCR + 4 * K + 512)
        fa = sb("fa", [P, SEQ], SCR + 6 * K)
        fb = sb("fb", [P, H_B, SEQ], SCR + 7 * K)
        t_lo = sb("t_lo", [P, 2, SEQ], SCR + 13 * K)
        gain_a = sb("gain_a", [P, D], SCR)
        junk = sb("junk", [P, D], SCR + 8 * K, BF16)
        rm_t = sb("rm_t", [P, SEQ], SCR + 12 * K)
        junk_o = sb("junk_o", [P, TB, P], SCR + 15 * K)
        up_lo = sb("up_lo", [P, 4, SEQ], SCR)
        up_u = sb("up_u", [P, 4, SEQ], SCR + 4 * K)
        up_c = sb("up_c", [P, 4, SEQ], SCR + 8 * K)
        up_g = sb("up_g", [P, 2, SEQ], SCR + 12 * K)
        up_a = sb("up_a", [P, 2, SEQ], SCR + 14 * K)
        off = [192 * K]

        def small(name, shape, dt=F32):
            t = sb(name, shape, off[0], dt)
            off[0] += (int(np.prod(shape[1:])) * 4 + 31) // 32 * 32
            return t

        bias = small("bias", [P, H_A, 384])
        mask_b = small("mask_b", [P, 384])
        mask_c = small("mask_c", [P, 384])
        ident = small("ident", [P, P])
        r_t = small("r_t", [P, SEQ])
        cols = small("cols", [P, NCOL])
        rows = small("rows", [P, NROW])
        ind = small("ind", [P, 384])
        h1_gains_all = small("h1_gains_all", [P, (DEPTH + 1) * KC])
        h1_gains = small("h1_gains", [P, KC])
        trig = small("trig", [P, 2, TB, HR])
        ang = small("ang", [P, TB, HR])
        kr = small("kr", [P, TB, D_ROPE])
        posq_i = small("posq_i", [P, TB], I32)
        posq = small("posq", [P, TB])
        ssq = small("ssq", [P, 32])
        var = small("var", [P, 32])
        nvar = small("nvar", [P, 32])
        rtmp = small("rtmp", [P, 32])
        rst = small("rst", [P, 32])
        rst_x = small("rst_x", [P, TB])
        rst_m = small("rst_m", [P, TB])
        ysum = small("ysum", [P, TB])
        xsq = small("xsq", [P, TB, 2])
        xsum = small("xsum", [P, TB])
        ysq = small("ysq", [P, TB, 4])
        lamv = small("lamv", [P, 8])
        nmax = small("nmax", [P, 4, TB])
        sums = small("sums", [P, 4, TB])
        rcp = small("rcp", [P, 4, TB])
        o_r = small("o_r", [P, TB, HEADS])
        o_sq = small("o_sq", [P, TB, HEADS])
        z_f = small("z_f", [P, TB, 2 * H_B])
        e_f = small("e_f", [P, TB, 2 * H_B])
        cw = small("cw", [P, 16])

        ps = ctx.enter_context(nc.psum_tensor("ps", [P, 8, 512], F32))
        lam_prod = rope_a
        lam_row = sb("lam_row", [P, 256], BIG + 19 * K)

        landed = [sem(f"landed{i}") for i in range(RAW)]
        hi_ready = sem("hi_ready")
        lo_ready = sem("lo_ready")
        split_free = sem("split_free")
        acc_free = [sem(f"acc_free{i}") for i in range(2)]
        t_lo_ready = sem("t_lo_ready")
        bank_done = sem("bank_done")
        bank_free = [sem(f"bank_free{i}") for i in range(4)]
        tsplit_hi = sem("tsplit_hi")
        x_here = [sem(f"x_here{i}") for i in range(4)]
        x_ready = sem("x_ready")
        x_sq = sem("x_sq")
        mem_sq = sem("mem_sq")
        lat_sq = sem("lat_sq")
        rstx_ready = sem("rstx_ready")
        rstm_ready = sem("rstm_ready")
        y_sq = sem("y_sq")
        y_half = sem("y_half")
        gain_here = sem("gain_here")
        par_here = sem("par_here")
        mem_here = sem("mem_here")
        first_here = sem("first_here")
        setup_pool = sem("setup_pool")
        setup_dve = sem("setup_dve")
        setup_act = sem("setup_act")
        tab_ready = sem("tab_ready")
        rst_ready = sem("rst_ready")
        up_sum = sem("up_sum")
        up_tap = sem("up_tap")
        bias_done = sem("bias_done")
        lam_prod_ready = sem("lam_prod_ready")
        lam_exp_ready = sem("lam_exp_ready")
        c_scaled = sem("c_scaled")
        k_cat_ready = sem("k_cat_ready")
        f_abs = sem("f_abs")
        f_exp = sem("f_exp")
        f_one = sem("f_one")
        f_ln = sem("f_ln")
        lf_ready = sem("lf_ready")
        fab_ready = sem("fab_ready")
        s_ready = sem("s_ready")
        p_ready = sem("p_ready")
        pn_ready = sem("pn_ready")
        osq_ready = sem("osq_ready")
        on_ready = sem("on_ready")
        xm_ready = sem("xm_ready")
        xpn_ready = sem("xpn_ready")
        up_free = [sem(f"up_free{i}") for i in range(2)]
        up_lo_ready = sem("up_lo_ready")
        up_aff_ready = sem("up_aff_ready")
        up_conv_ready = sem("up_conv_ready")
        up_gelu_ready = sem("up_gelu_ready")
        up_mul_ready = sem("up_mul_ready")
        up_hi_ready = sem("up_hi_ready")
        act_ready = sem("act_ready")
        cw_ready = sem("cw_ready")
        gate = sem("gate")
        stored = sem("stored")
        dve_step = sem("dve_step")
        pool_step = sem("pool_step")

        def acc_read(l, g):
            return acc_free[g % 2], l * (NGROUPS // 2) + (g // 2 + 2)

        def item_read(l, item):
            w = ITEM[item]
            return bank_free[w % 4], l * (NITEMS // 4) + (H1_BEFORE // 4 + w // 4 + 2)

        def item_done(l, item):
            return bank_done, l * NITEMS + (H1_BEFORE + ITEM[item] + 1)

        def x_block(l, k, i):
            return x_ready, l * 24 + (8 + 8 * k + i + 1)

        def pieces_used(l, p):
            return split_free, l * NPIECES + (SPL + p)

        def score_tile_slot(n):
            return JOB[(n, 0)] % 3

        def acc(g, b):
            return ps[:, 2 * (g % 2) + b, :]

        def bank(item):
            return ps[:, 4 + ITEM[item] % 4, :]

        def tsplit_job(item):
            kind, i = item
            two = [2 * i, 2 * i + 1]
            if kind == "h1":
                return h_t, two, [h1_gains[:, c:c + 1] for c in two]
            if kind == "h2":
                return h2_t, two, [cols[:, CG2 + c:CG2 + c + 1] for c in two]
            if kind == "h3":
                return h_t, two, [cols[:, CG4 + c:CG4 + c + 1] for c in two]
            if kind == "mem_T":
                return m_t, two, [cols[:, CMEM + c:CMEM + c + 1] for c in two]
            if kind == "head_T":
                heads = HEAD_ORDER[2 * i:2 * i + 2]
                return o_t, heads, [cols[:, CHEAD + h:CHEAD + h + 1] for h in heads]
            if kind == "latent_T":
                return c_t, LATENT_CHUNKS[i], [cols[:, CQN + c:CQN + c + 1] for c in LATENT_CHUNKS[i]]
            return xo_t, [i], None

        block = ctx.enter_context(nc.Block())

        @block.sync
        def _(sp):
            sp.dma_start(posk_i[:], pos_in.partition_broadcast(P)).then_inc(first_here, 16)
            sp.dma_start(posq_i[:], posq_in).then_inc(first_here, 16)
            xs = x_in.rearrange("(t p) d -> p t d", p=P)
            for j in range(RAW):
                if j < 4:
                    cs = slice(512 * j, 512 * j + 512)
                    sp.dma_start(x[:, :, cs], xs[:, :, cs]).then_inc(x_here[j], 16)
                sp.dma_start(raw[:, j, :], stream[j]).then_inc(landed[j], 16)
            with sp.Fori(1, DEPTH * NPIECES // RAW) as r:
                for j in range(RAW):
                    sp.wait_ge(lo_ready, r * RAW + (j + 1 - RAW))
                    sp.dma_start(raw[:, j, :], stream[r * RAW + j]).then_inc(landed[j], 16)
            for j in range(SPL):
                sp.wait_ge(lo_ready, DEPTH * NPIECES + j + 1 - RAW)
                sp.dma_start(raw[:, j, :], stream[DEPTH * NPIECES + j]).then_inc(landed[j], 16)
            for j in range(SPL):
                sp.wait_ge(landed[j], 16 * (DEPTH * NPIECES // RAW + 1))
            for i in range(4):
                sp.wait_ge(*x_block(DEPTH - 1, 2, 2 * i + 1))
                cs = slice(512 * i, 512 * i + 512)
                sp.dma_start(out.rearrange("(t p) d -> p t d", p=P)[:, :, cs], x[:, :, cs]).then_inc(stored, 16)
            sp.wait_ge(stored, 64)

        @block.tensor
        def _(pe):
            pe.sem_inc(split_free, SPL)

            def x_transposes(b, i):
                for kk in range(2):
                    for tb in range(TB):
                        mm = pe.transpose(b[:, kk * SEQ + tb * P:kk * SEQ + (tb + 1) * P],
                                          x[:, tb, (2 * i + kk) * P:(2 * i + kk + 1) * P], ident[:])
                mm.then_inc(bank_done, 1)

            pe.wait_ge(setup_pool, 1)
            for i in range(H1_BEFORE):
                pe.wait_ge(x_here[i // 2], 16)
                pe.wait_ge(bank_free[i % 4], i // 4 + 1)
                x_transposes(ps[:, 4 + i % 4, :], i)

            with pe.Fori(0, DEPTH) as l:
                def take_bank(item):
                    w = ITEM[item]
                    pe.wait_ge(bank_free[w % 4], l * (NITEMS // 4) + (H1_BEFORE // 4 + w // 4 + 1))
                    return bank(item)

                def take_acc(g, g_count=None):
                    pe.wait_ge(acc_free[g % 2], l * (NGROUPS // 2) + (g // 2 + 1 if g_count is None else g_count))

                def take_piece(p):
                    pe.wait_ge(lo_ready, l * NPIECES + p + 1)

                def nat_mm(g, slot, c0, src, chunks, width, first, last, col=0, woff=0):
                    hi = w_hi[:, slot, woff:woff + len(chunks) * width].rearrange("p (c n) -> p c n", n=width)
                    lo = w_lo[:, slot, woff:woff + len(chunks) * width].rearrange("p (c n) -> p c n", n=width)
                    for j, c in enumerate(chunks):
                        f, e = first and j == 0, last and j == len(chunks) - 1
                        for tb in range(TB):
                            dst = acc(g, tb)[:, col:col + width]
                            s_hi = src[:, c, 0, tb * P:(tb + 1) * P]
                            s_lo = src[:, c, 1, tb * P:(tb + 1) * P]
                            pe.matmul(dst, s_hi, hi[:, j, :], start=f, stop=False, skip_group_check=True)
                            pe.matmul(dst, s_hi, lo[:, j, :], start=False, stop=False, skip_group_check=True)
                            mm = pe.matmul(dst, s_lo, hi[:, j, :], start=False, stop=e, skip_group_check=True)
                    return mm

                def t_mm(g, slot, src, chunks, first, last):
                    hi = w_hi[:, slot, :].rearrange("p (c n) -> p c n", n=256)
                    lo = w_lo[:, slot, :].rearrange("p (c n) -> p c n", n=256)
                    for j, c in enumerate(chunks):
                        f, e = first and j == 0, last and j == len(chunks) - 1
                        for nt in range(2):
                            dst = acc(g, nt)
                            pe.matmul(dst, hi[:, j, nt * P:(nt + 1) * P], src[:, c, :, :],
                                      start=f, stop=False, skip_group_check=True)
                            mm = pe.matmul(dst[:, SEQ:2 * SEQ], lo[:, j, nt * P:(nt + 1) * P], src[:, c, 0, :],
                                           start=False, stop=e, skip_group_check=True)
                    return mm

                def tile_ready(item):
                    pe.wait_ge(*item_read(l, item))

                def w_in_piece(p):
                    gi, j = piece_group(p)
                    name, kind, n, ch, width = W_IN_GROUPS[gi]
                    if j == 0:
                        take_acc(gi)
                    take_piece(p)
                    if kind == "T":
                        mm = t_mm(gi, p % SPL, h_t, range(4 * j, 4 * j + 4), j == 0, j == n - 1)
                    elif name == "uqa":
                        tile_ready(("latent_T", 2))
                        mm = nat_mm(gi, p % SPL, 0, c_t, [2 * j, 2 * j + 1], 512, j == 0, j == 1)
                    elif name == "small":
                        tile_ready(("latent_T", 4))
                        if j < 2:
                            mm = nat_mm(gi, p % SPL, 0, c_t, [2 * j, 2 * j + 1], 64, j == 0, j == 1)
                        else:
                            mm = nat_mm(gi, p % SPL, 0, c_t, [2 + j], 128, j == 2, j == 3, col=64)
                    elif name.startswith("ukv"):
                        mm = nat_mm(gi, p % SPL, 0, c_t, [4, 5], 512, True, True)
                    else:
                        if gi == 0:
                            if j < H1_BEFORE:
                                pe.wait_ge(bank_free[j], l * (NITEMS // 4) + 2)
                            else:
                                tile_ready(("h1", j))
                        mm = nat_mm(gi, p % SPL, 0, h_t, [2 * j, 2 * j + 1], width, j == 0, j == n - 1)
                    mm.then_inc(split_free, 1)

                def up_piece(half, j, p):
                    take_piece(p)
                    hi = w_hi[:, j % SPL, :].rearrange("p (c n) -> p c n", n=512)
                    lo = w_lo[:, j % SPL, :].rearrange("p (c n) -> p c n", n=512)
                    for cc in range(2):
                        c = 2 * j + cc
                        for nt in range(4):
                            dst = ps[:, 4 * half + nt, :]
                            pe.matmul(dst, hi[:, cc, nt * P:(nt + 1) * P], h_t[:, c, :, :],
                                      start=(c == 0), stop=False, skip_group_check=True)
                            mm = pe.matmul(dst[:, SEQ:2 * SEQ], lo[:, cc, nt * P:(nt + 1) * P], h_t[:, c, 0, :],
                                           start=False, stop=(c == KC - 1), skip_group_check=True)
                    mm.then_inc(split_free, 1)

                def piece(p):
                    if p < P_OUT:
                        w_in_piece(p)
                    elif p < P_MEMK:
                        k, j = OUT_ORDER[p - P_OUT]
                        if j == 0:
                            take_acc(G_OUT + k)
                        take_piece(p)
                        tile_ready(("head_T", j))
                        nat_mm(G_OUT + k, p % SPL, 0, o_t, HEAD_ORDER[2 * j:2 * j + 2], 512, j == 0, j == 7).then_inc(split_free, 1)
                    elif p < P_MEMV:
                        k, j = (p - P_MEMK) // 4, (p - P_MEMK) % 4
                        src, tiles = (m_t, "mem_T") if k < 2 else (h2_t, "h2")
                        if j == 0:
                            take_acc(G_MEMK + k)
                        take_piece(p)
                        for t in range(2):
                            tile_ready((tiles, 2 * j + t))
                        t_mm(G_MEMK + k, p % SPL, src, range(4 * j, 4 * j + 4), j == 0, j == 3).then_inc(split_free, 1)
                    elif p < P_WO:
                        j = p - P_MEMV
                        if j == 0:
                            take_acc(G_MEMV)
                        take_piece(p)
                        nat_mm(G_MEMV, p % SPL, 0, m_t, [2 * j, 2 * j + 1], 512, j == 0, j == 7).then_inc(split_free, 1)
                    elif p < P_UP:
                        k, j = (p - P_WO) // 2, (p - P_WO) % 2
                        if j == 0:
                            take_acc(G_WO + k)
                        take_piece(p)
                        tile_ready(("XO", 2 * j + 1))
                        nat_mm(G_WO + k, p % SPL, 0, xo_t, [2 * j, 2 * j + 1], 512, j == 0, j == 1).then_inc(split_free, 1)
                    else:
                        j = p - P_UP
                        if j == 0:
                            for g in (G_WO + 2, G_WO + 3):
                                pe.wait_ge(*acc_read(l, g))
                            pe.wait_ge(up_free[0], l * (UPG // 2) + 1)
                        tile_ready(("h3", j))
                        up_piece(0, j, p)

                def x_tile(step):
                    kind, i = step
                    if kind == "h1" and i >= H1_BEFORE:
                        pe.wait_ge(x_here[i // 2], 16)
                        pe.wait_ge(x_ready, l * 24 + 8)
                    else:
                        pe.wait_ge(*x_block(l, {"h2": 0, "h3": 1, "h1": 2}[kind], i))
                    x_transposes(take_bank(step), i)

                for step in STEPS:
                    kind = step[0]
                    if kind == "mm":
                        piece(step[1])
                    elif kind in ("h1", "h2", "h3"):
                        x_tile(step)
                    elif kind == "mem_T":
                        i = step[1]
                        pe.wait_ge(mem_here, l * 16 + 16)
                        b = take_bank(step)
                        for kk in range(2):
                            for tb in range(TB):
                                mm = pe.transpose(b[:, kk * SEQ + tb * P:kk * SEQ + (tb + 1) * P],
                                                  m_nat[:, tb, (2 * i + kk) * P:(2 * i + kk + 1) * P], ident[:])
                        mm.then_inc(bank_done, 1)
                    elif kind == "R":
                        if step[1] == "mem":
                            pe.wait_ge(rstm_ready, l + 1)
                        else:
                            pe.wait_ge(rstx_ready, l * 3 + int(step[1][1]))
                        src = rst_m if step[1] == "mem" else rst_x
                        b = take_bank(step)
                        for tb in range(TB):
                            mm = pe.matmul(b[:, tb * P:(tb + 1) * P], src[:, tb:tb + 1].to_broadcast([P, P]), ident[:],
                                           start=True, stop=True)
                        mm.then_inc(bank_done, 1)
                    elif kind == "XS":
                        h = step[1]
                        pe.wait_ge(*acc_read(l, G_MEMK + h // 2))
                        pe.wait_ge(*acc_read(l, G_WQ + h // 2))
                        b = take_bank(step)
                        for tb in range(TB):
                            mm = pe.matmul(b[:, tb * SEQ:(tb + 1) * SEQ], qx_t[:, h, tb * P:(tb + 1) * P], kx_t[:, h, :],
                                           start=True, stop=True)
                        mm.then_inc(bank_done, 1)
                    elif kind == "XT":
                        h = step[1]
                        pe.wait_ge(xpn_ready, l * H_X + h + 1)
                        b = take_bank(step)
                        for kb in range(2):
                            for tb in range(TB):
                                mm = pe.transpose(b[:, kb * SEQ + tb * P:kb * SEQ + (tb + 1) * P],
                                                  px[:, h, tb, kb * P:(kb + 1) * P], ident[:])
                        mm.then_inc(bank_done, 1)
                    elif kind == "XO":
                        h = step[1]
                        pe.wait_ge(*acc_read(l, G_MEMV))
                        pe.wait_ge(*item_read(l, ("XT", h)))
                        b = take_bank(step)
                        for kb in range(2):
                            mm = pe.matmul(b[:, 0:SEQ], vx[:, kb, h * P:(h + 1) * P], px_t[:, h, kb, :],
                                           start=(kb == 0), stop=(kb == 1))
                        mm.then_inc(bank_done, 1)
                    elif kind == "latent_T":
                        pe.wait_ge(c_scaled, l + 1)
                        b = take_bank(step)
                        for kk, c in enumerate(LATENT_CHUNKS[step[1]]):
                            src = cq[:, :, c * P:(c + 1) * P] if c < 4 else ckv[:, :, (c - 4) * P:(c - 3) * P]
                            for tb in range(TB):
                                mm = pe.transpose(b[:, kk * SEQ + tb * P:kk * SEQ + (tb + 1) * P], src[:, tb, :], ident[:])
                        mm.then_inc(bank_done, 1)
                    elif kind == "latent_qk_T":
                        h = step[1]
                        pe.wait_ge(k_cat_ready, l + 1)
                        b = take_bank(step)
                        for a, src in enumerate((q_nat, k_cat)):
                            for tb in range(TB):
                                mm = pe.transpose(b[0:DQ_C, a * SEQ + tb * P:a * SEQ + (tb + 1) * P], src[:, tb, h, :], ident[:])
                        mm.then_inc(bank_done, 1)
                    elif kind == "forget_scan":
                        pe.wait_ge(lf_ready, l + 1)
                        b = take_bank(step)
                        for tb in range(TB):
                            mm = pe.transpose(b[0:2 * H_B, tb * P:(tb + 1) * P], z_f[:, tb, :], ident[:])
                        mm.then_inc(bank_done, 1)
                    elif kind == "S":
                        hk, h = HEAD_SEQ[step[1]]
                        if hk == "A":
                            pe.wait_ge(*acc_read(l, GROUP[f"qa{h // 2}"]))
                            pe.wait_ge(*acc_read(l, GROUP[f"ka{h // 2}"]))
                        elif hk == "B":
                            pe.wait_ge(*acc_read(l, GROUP[f"qb{h // 2}"]))
                            pe.wait_ge(*acc_read(l, GROUP[f"kb{h // 2}"]))
                            pe.wait_ge(fab_ready, l + 1)
                        else:
                            pe.wait_ge(*item_read(l, ("latent_qk_T", h)))
                        for job in jobs_of(step[1]):
                            b = take_bank(("S", job))
                            m = job[1]
                            for tb, (o, nk) in enumerate(((0, P), (P, SEQ))):
                                dst, q = b[:, o:o + nk], slice(tb * P, (tb + 1) * P)
                                if hk == "A":
                                    r = slice(m * DK_A, (m + 1) * DK_A)
                                    mm = pe.matmul(dst, qa_t[r, h, q], ka_t[r, h, 0:nk], start=True, stop=True)
                                elif hk == "B":
                                    pe.matmul(dst, qb_t[:, h, q], kb_t[:, h, 0:nk], start=True, stop=False)
                                    mm = pe.matmul(dst, fa[0:2 * H_B, q], fb[0:2 * H_B, h, 0:nk], start=False, stop=True)
                                else:
                                    mm = pe.matmul(dst, qc_t[0:DQ_C, h, q], kc_t[0:DQ_C, h, 0:nk], start=True, stop=True)
                            mm.then_inc(bank_done, 1)
                    elif kind == "T":
                        n = step[1]
                        slot = score_tile_slot(n)
                        if HEAD_SEQ[n][0] == "A":
                            pe.wait_ge(pn_ready, l * H_A + HEAD_SEQ[n][1] + 1)
                        else:
                            pe.wait_ge(p_ready, l * len(JOB) + JOB[(n, 0)] + 1)
                        b = take_bank(step)
                        for t, o in enumerate((0, P, 2 * P)):
                            mm = pe.transpose(b[:, t * P:(t + 1) * P], s_sb[:, slot, o:o + P], ident[:])
                        mm.then_inc(bank_done, 1)
                    elif kind == "O":
                        n = step[1]
                        hk, h = HEAD_SEQ[n]
                        v = {"A": va, "B": vb, "C": vc}[hk]
                        for name in {"A": ["va"], "B": ["vb", "vbf"], "C": ["small", "ukv0", "ukv1"]}[hk]:
                            pe.wait_ge(*acc_read(l, GROUP[name]))
                        pe.wait_ge(*item_read(l, ("T", n)))
                        b = take_bank(step)
                        vh = v[:, :, h * P:(h + 1) * P]
                        pe.matmul(b[:, 0:P], p_t[:, 0:P], vh[:, 0, :], start=True, stop=True)
                        pe.matmul(b[:, P:2 * P], p_t[:, P:2 * P], vh[:, 0, :], start=True, stop=False, skip_group_check=True)
                        mm = pe.matmul(b[:, P:2 * P], p_t[:, 2 * P:3 * P], vh[:, 1, :], start=False, stop=True,
                                       skip_group_check=True)
                        mm.then_inc(bank_done, 1)
                    elif kind == "head_T":
                        i = step[1]
                        pe.wait_ge(on_ready, l * 3 + (1 if i < 3 else 2 if i < 6 else 3))
                        b = take_bank(step)
                        for kk in range(2):
                            h = HEAD_ORDER[2 * i + kk]
                            for tb in range(TB):
                                mm = pe.transpose(b[:, kk * SEQ + tb * P:kk * SEQ + (tb + 1) * P],
                                                  o_nat[:, tb, h * P:(h + 1) * P], ident[:])
                        mm.then_inc(bank_done, 1)

                for b in range(4):
                    last = max(ITEM[s] for s in ITEMS if s[0] != "h1" and ITEM[s] % 4 == b)
                    pe.wait_ge(*item_read(l, ITEMS[last]))
                pe.sem_inc(gate, 1)
                with pe.Fori(0, UPG // 2 - 1) as i:
                    for half in (1, 0):
                        pe.wait_ge(up_free[half], l * (UPG // 2) + i + (2 - half))
                        for j in range(8):
                            up_piece(half, j, i * 16 + (P_UP + 8 * (2 - half) + j))
                pe.wait_ge(up_free[1], l * (UPG // 2) + UPG // 2)
                for j in range(8):
                    up_piece(1, j, P_DOWN - 8 + j)
                pe.wait_ge(up_free[0], l * (UPG // 2) + UPG // 2 + 1)
                pe.sem_inc(gate, 1)
                with pe.Fori(0, 2) as i:
                    for k in range(2):
                        g = G_DOWN + k
                        take_acc(g, i + (g // 2 + 1))
                        for j in range(16):
                            take_piece(i * 32 + (P_DOWN + 16 * k + j))
                            if k == 0:
                                pe.wait_ge(act_ready, l * UPG + j + 1)
                            nat_mm(g, j % SPL, 0, act_t, [2 * j, 2 * j + 1], 512, j == 0, j == 15).then_inc(split_free, 1)
                pe.wait_ge(up_free[1], l * (UPG // 2) + UPG // 2 + 1)
                for step in END_STEPS:
                    if step[0] == "h1":
                        x_tile(step)
    
        @block.scalar
        def _(act):
            def split_hi(slot, rslot, landed_count, piece_count, width=PW):
                act.wait_ge(landed[rslot], landed_count)
                act.wait_ge(split_free, piece_count)
                act.activation(w_hi[:, slot, 0:width], raw[:, rslot, 0:width], ACT.Copy).then_inc(hi_ready, 1)

            act.dma_start(first_row[:], first_row_in.partition_broadcast(P)).then_inc(first_here, 16)
            act.dma_start(h1_gains_all[:], h1_gains_in).then_inc(first_here, 16)

            def hi_tile(dst, chunks, gains, b):
                for kk, c in enumerate(chunks):
                    kw = {} if gains is None else {"scale": gains[kk]}
                    ins = act.activation(dst[:, c, 0, :], b[:, kk * SEQ:(kk + 1) * SEQ], ACT.Copy, **kw)
                ins.then_inc(tsplit_hi, 1)

            act.wait_ge(setup_dve, 1)
            for i in range(H1_BEFORE):
                act.wait_ge(bank_done, i + 1)
                hi_tile(*tsplit_job(("h1", i)), ps[:, 4 + i % 4, :])
                if i < SPL:
                    split_hi(i, i, 16, i + 1, piece_width(i))
            act.wait_ge(setup_dve, 2)
            act.activation(trig[:], trig[:], ACT.Sin).then_inc(setup_act, 1)

            with act.Fori(0, DEPTH) as l:
                def split(p):
                    w = piece_width(p % NPIECES)
                    split_hi(p % SPL, p % RAW, (l * (NPIECES // RAW) + p // RAW + 1) * 16, l * NPIECES + p + 1, w)

                def split_dyn(p0, j, i, per):
                    q = p0 + j
                    split_hi(q % SPL, q % RAW, (l * (NPIECES // RAW) + i * (per // RAW) + (q // RAW + 1)) * 16,
                             l * NPIECES + i * per + (q + 1))

                def read_bank(item):
                    act.wait_ge(*item_done(l, item))
                    return bank(item)

                def free_bank(ins, item):
                    ins.then_inc(bank_free[ITEM[item] % 4], 1)

                def tsplit(item):
                    b = read_bank(item)
                    hi_tile(*tsplit_job(item), b)

                def group_done(g, dyn=0):
                    act.wait_ge(*pieces_used(l, dyn + GROUP_END[g]))

                def x_stats(k, half):
                    act.wait_ge(x_ready, l * 24 + (4 + 4 * half + 8 * k))
                    if half == 1:
                        act.wait_ge(x_sq, l * 6 + (2 * k + 1))
                    for tb in range(TB):
                        ins = act.activation(junk[:, 1024 * tb:1024 * tb + 1024], x[:, tb, 1024 * half:1024 * half + 1024],
                                             ACT.Square, accum_out=xsq[:, tb, half:half + 1])
                    ins.then_inc(x_sq, 1)

                def t_evac_lo(g):
                    group_done(g)
                    if T_BEFORE[g] is not None:
                        act.wait_ge(*acc_read(l, T_BEFORE[g]))
                    act.activation(t_lo[:], ps[:, 2 * (g % 2):2 * (g % 2) + 2, SEQ:2 * SEQ], ACT.Copy).then_inc(t_lo_ready, 1)

                def y_squares(g, yk):
                    group_done(g)
                    if yk > 0:
                        act.wait_ge(y_sq, l * 24 + 2 * yk)
                    for tb in range(TB):
                        if tb == 1:
                            act.wait_ge(y_half, l * 12 + yk + 1)
                        act.activation(junk[:, 512 * tb:512 * tb + 512], acc(g, tb), ACT.Square,
                                       accum_out=ysq[:, tb, yk % 4:yk % 4 + 1]).then_inc(y_sq, 1)

                act.wait_ge(x_ready, l * 24 + 8)
                act.dma_start(cols[:], cols_in[l]).then_inc(par_here, 16)
                act.dma_start(rows[:], rows_in[l].partition_broadcast(P)).then_inc(par_here, 16)
                act.dma_start(lam_row[:], lam_in[l].partition_broadcast(P)).then_inc(par_here, 16)

                for step in STEPS:
                    kind = step[0]
                    if kind == "split":
                        split(step[1])
                    elif kind == "evac":
                        gi = step[1]
                        if G_OUT <= gi < G_MEMK:
                            y_squares(gi, gi - G_OUT)
                            continue
                        if G_WO <= gi < G_DOWN:
                            y_squares(gi, 4 + gi - G_WO)
                            continue
                        if gi == G_MEMV:
                            group_done(gi)
                            act.wait_ge(rstm_ready, l + 1)
                            for tb in range(TB):
                                ins = act.activation(vx[:, tb, :], acc(gi, tb), ACT.Copy, scale=rst_m[:, tb:tb + 1])
                            ins.then_inc(acc_free[gi % 2], 1)
                            continue
                        if gi >= G_MEMK:
                            t_evac_lo(gi)
                            continue
                        name = W_IN_GROUPS[gi][0]
                        if W_IN_GROUPS[gi][1] == "T":
                            t_evac_lo(gi)
                            continue
                        group_done(gi)
                        scaled = name in ("cq", "ckv", "vbf", "vb", "va")
                        if scaled:
                            act.wait_ge(rstx_ready, l * 3 + 1)
                        moves = []
                        for tb in range(TB):
                            a = acc(gi, tb)
                            if name == "cq":
                                moves.append((tb, cq[:, tb, :], a[:, 0:512]))
                            elif name == "ckv":
                                moves.append((tb, ckv[:, tb, :], a[:, 0:288]))
                            elif name == "uqa":
                                moves.append((tb, q_nat[:, tb].rearrange("p h d -> p (h d)")[:, 0:512], a[:, 0:512]))
                            elif name == "small":
                                moves.append((tb, q_nat[:, tb].rearrange("p h d -> p (h d)")[:, 512:576], a[:, 0:64]))
                                moves.append((tb, vc[:, tb, 640:768], a[:, 64:192]))
                            elif name == "ukv0":
                                kv = a[:, 0:384].rearrange("p (h d) -> p h d", d=192)
                                moves.append((tb, k_cat[:, tb, 0:2, 0:64], kv[:, :, 0:64]))
                                moves.append((tb, vc[:, tb, 0:256].rearrange("p (h d) -> p h d", d=P), kv[:, :, 64:192]))
                                moves.append((tb, k_cat[:, tb, 2, 0:64], a[:, 384:448]))
                                moves.append((tb, vc[:, tb, 256:320], a[:, 448:512]))
                            elif name == "ukv1":
                                moves.append((tb, vc[:, tb, 320:384], a[:, 0:64]))
                                kv = a[:, 64:448].rearrange("p (h d) -> p h d", d=192)
                                moves.append((tb, k_cat[:, tb, 3:5, 0:64], kv[:, :, 0:64]))
                                moves.append((tb, vc[:, tb, 384:640].rearrange("p (h d) -> p h d", d=P), kv[:, :, 64:192]))
                                moves.append((tb, k_cat[:, tb, 5, 0:64], a[:, 448:512]))
                            elif name == "va":
                                moves.append((tb, va[:, tb, :], a[:, 0:512]))
                            elif name == "vbf":
                                moves.append((tb, vb[:, tb, 512:768], a[:, 0:256]))
                                moves.append((tb, z_f[:, tb, :], a[:, 256:256 + 2 * H_B]))
                            elif name == "vb":
                                moves.append((tb, vb[:, tb, 0:512], a[:, 0:512]))
                        for tb, dst, src in moves:
                            kw = {"scale": rst_x[:, tb:tb + 1]} if scaled else {}
                            ins = act.activation(dst, src, ACT.Copy, **kw)
                        ins.then_inc(acc_free[gi % 2], 1)
                    elif step == ("latent", "squares"):
                        act.wait_ge(*acc_read(l, GROUP["ckv"]))
                        act.wait_ge(x_sq, l * 6 + 2)
                        act.wait_ge(par_here, l * 48 + 48)
                        for tb in range(TB):
                            act.activation(junk[:, tb * 512:tb * 512 + 512], cq[:, tb, :], ACT.Square, accum_out=ssq[:, tb:tb + 1])
                        for tb in range(TB):
                            ins = act.activation(junk[:, 1024 + tb * 256:1280 + tb * 256], ckv[:, tb, 0:256], ACT.Square,
                                                 accum_out=ssq[:, 2 + tb:3 + tb])
                        ins.then_inc(lat_sq, 1)
                    elif step == ("latent", "scale"):
                        act.wait_ge(rst_ready, l + 1)
                        for tb in range(TB):
                            act.activation(cq[:, tb, :], cq[:, tb, :], ACT.Copy, scale=rst[:, tb:tb + 1])
                        for tb in range(TB):
                            ins = act.activation(ckv[:, tb, 0:256], ckv[:, tb, 0:256], ACT.Copy, scale=rst[:, 2 + tb:3 + tb])
                        ins.then_inc(c_scaled, 1)
                    elif kind in ("latent_T", "head_T", "mem_T", "h1", "h2", "h3", "XO"):
                        tsplit(step)
                    elif kind == "x_stats":
                        x_stats(*step[1:])
                    elif kind == "lam":
                        act.wait_ge(lam_prod_ready, l + 1)
                        act.activation(lamv[:, 2:4], lamv[:, 0:2], ACT.Exp).then_inc(lam_exp_ready, 1)
                    elif kind == "R":
                        b = read_bank(step)
                        free_bank(act.activation((rm_t if step[1] == "mem" else r_t)[:], b[:, 0:SEQ], ACT.Copy), step)
                    elif kind == "osq":
                        n = step[1]
                        hk, h = HEAD_SEQ[n]
                        col = {"A": 0, "B": H_A, "C": H_A + H_B}[hk] + h
                        act.wait_ge(*item_read(l, ("O", n)))
                        if n > 0:
                            act.wait_ge(osq_ready, l * HEADS + n)
                        for tb in range(TB):
                            ins = act.activation(junk_o[:, tb, :], o_nat[:, tb, col * P:(col + 1) * P], ACT.Square,
                                                 accum_out=o_sq[:, tb, col:col + 1])
                        ins.then_inc(osq_ready, 1)
                    elif kind == "load_gain":
                        if step[1] == 0:
                            act.wait_ge(*item_done(l, ("O", HEADS - 1)))
                        else:
                            act.wait_ge(*acc_read(l, G_OUT + 3))
                        act.dma_start(gain_a[:], gains_in[l * 3 + step[1]].partition_broadcast(P)).then_inc(gain_here, 16)
                    elif kind == "load_mem":
                        act.wait_ge(*item_done(l, ("head_T", 7)))
                        act.dma_start(m_nat[:], mem_in.rearrange("(t p) d -> p t d", p=P)).then_inc(mem_here, 16)
                    elif kind == "mem_stats":
                        tb = step[1]
                        act.wait_ge(mem_here, l * 16 + 16)
                        act.wait_ge(y_sq, l * 24 + 4)
                        if tb == 1:
                            act.wait_ge(mem_sq, l * 2 + 1)
                        act.activation(junk[:], m_nat[:, tb, :], ACT.Square, accum_out=ssq[:, tb:tb + 1]).then_inc(mem_sq, 1)
                    elif kind == "XS":
                        h = step[1]
                        act.wait_ge(xm_ready, l * H_X + h + 1)
                        b = bank(step)
                        for tb in range(TB):
                            ins = act.activation(px[:, h, tb, :], b[:, tb * SEQ:(tb + 1) * SEQ], ACT.Exp,
                                                 bias=nmax[:, h, tb:tb + 1], scale=float(D_X ** -0.5),
                                                 accum_out=sums[:, h, tb:tb + 1])
                        free_bank(ins, step)
                    elif kind == "XT":
                        b = read_bank(step)
                        free_bank(act.activation(px_t[:, step[1]].rearrange("p a b -> p (a b)"), b, ACT.Copy), step)
                    elif kind == "latent_qk_T":
                        h = step[1]
                        b = read_bank(step)
                        if h == 0:
                            act.wait_ge(tab_ready, 1)
                        act.activation(qc_t[0:DQ_C, h, :], b[0:DQ_C, 0:SEQ], ACT.Copy)
                        free_bank(act.activation(kc_t[0:DQ_C, h, :], b[0:DQ_C, SEQ:2 * SEQ], ACT.Copy), step)
                    elif step == ("forget", "exp"):
                        act.wait_ge(f_abs, l + 1)
                        act.activation(e_f[:], e_f[:], ACT.Exp, scale=-1.0).then_inc(f_exp, 1)
                    elif step == ("forget", "ln"):
                        act.wait_ge(f_one, l + 1)
                        act.activation(e_f[:], e_f[:], ACT.Ln).then_inc(f_ln, 1)
                    elif kind == "S":
                        for job in jobs_of(step[1]):
                            j = JOB[job]
                            act.wait_ge(s_ready, l * len(JOB) + j + 1)
                            for tb, (o, nk) in enumerate(((0, P), (P, SEQ))):
                                ins = act.activation(s_sb[:, j % 3, o:o + nk], s_sb[:, j % 3, o:o + nk], ACT.Exp,
                                                     bias=nmax[:, j % 4, tb:tb + 1], accum_out=sums[:, j % 4, tb:tb + 1])
                            ins.then_inc(p_ready, 1)
                    elif kind == "T":
                        n = step[1]
                        b = read_bank(step)
                        if n >= 1:
                            act.wait_ge(*item_done(l, ("O", n - 1)))
                        free_bank(act.activation(p_t[:], b[:, 0:384], ACT.Copy), step)
                def up_split(i, half, j):
                    split_dyn(P_UP + 8 * half + SPL, j, i, 16)

                def up_tail(i, half, j):
                    g = i * 2 + half
                    if j == 0:
                        act.wait_ge(*pieces_used(l, i * 16 + (P_UP + 8 * half + 8)))
                        act.wait_ge(up_free[1 - half], l * (UPG // 2) + i + (1 + half))
                        act.activation(up_lo[:], ps[:, 4 * half:4 * half + 4, SEQ:2 * SEQ], ACT.Copy).then_inc(up_lo_ready, 1)
                    if j == 3:
                        act.wait_ge(up_conv_ready, l * UPG + g + 1)
                        act.activation(up_g[:], up_c[:, 0:2, :], ACT.Gelu_apprx_tanh).then_inc(up_gelu_ready, 1)
                    if j == 5:
                        act.wait_ge(up_mul_ready, l * UPG + g + 2)
                        act.activation(act_t[:, bass.ds(2 * g, 2), 0, :], up_a[:], ACT.Copy).then_inc(up_hi_ready, 1)

                with act.Fori(0, UPG // 2 - 1) as i:
                    for j in range(8):
                        up_split(i, 1, j)
                        up_tail(i, 0, j)
                    for j in range(8):
                        split_dyn(P_UP + 16 + SPL, j, i, 16)
                        up_tail(i, 1, j)
                for j in range(8):
                    up_split(UPG // 2 - 1, 1, j)
                    up_tail(UPG // 2 - 1, 0, j)
                for j in range(8):
                    split(P_DOWN + SPL + j)
                    up_tail(UPG // 2 - 1, 1, j)
                act.wait_ge(*pieces_used(l, P_DOWN))
                act.dma_start(gain_f[:], gains_in[l * 3 + 2].partition_broadcast(P)).then_inc(gain_here, 16)
                for j in range(8, 16):
                    split(P_DOWN + SPL + j)
                for k in range(1, 4):
                    y_squares(G_DOWN + k - 1, 8 + k - 1)
                    for j in range(16):
                        if (k, j) != (3, 15):
                            split(P_DOWN + 16 * k + SPL + j)
                y_squares(G_DOWN + 3, 11)
                for step in END_STEPS:
                    if step[0] == "h1":
                        tsplit(step)
                    if step == ("h1", 0):
                        split(NPIECES - 1 + SPL)

        @block.vector
        def _(dve):
            st = Steps(dve, dve_step)

            def split_lo(slot, rslot, count, width=PW):
                dve.wait_ge(hi_ready, count)
                dve.tensor_tensor(w_lo[:, slot, 0:width], raw[:, rslot, 0:width],
                                  w_hi[:, slot, 0:width].bitcast(F32), ALU.subtract).then_inc(lo_ready, 1)

            dve.sem_inc(up_mul_ready, 1)
            for s in range(2):
                dve.sem_inc(acc_free[s], 1)
                dve.sem_inc(up_free[s], 1)
            for b in range(4):
                dve.sem_inc(bank_free[b], 1)
            dve.wait_ge(first_here, 64)
            dve.tensor_copy(posk[:], posk_i[:])
            st.done(dve.tensor_copy(posq[:], posq_i[:]))
            st.done(dve.tensor_copy(h1_gains[:], h1_gains_all[:, 0:KC]))
            dve.sem_inc(setup_dve, 1)
            dve.tensor_scalar(rel[:, 0:P], posk[:, 0:P], posq[:, 0:1], None, ALU.subtract)
            dve.tensor_scalar(rel[:, P:384], posk[:], posq[:, 1:2], None, ALU.subtract)
            dve.tensor_tensor(dtab[:, 0:15, :], tab[:, 0:15, :], tab[:, 1:16, :], ALU.subtract)
            dve.tensor_tensor(dtab[:, 15:16, :], tab[:, 17:18, :], tab[:, 0:1, :], ALU.subtract)
            st.done(dve.tensor_tensor(dtab[:, 16:30, :], tab[:, 18:32, :], tab[:, 17:31, :], ALU.subtract))
            dve.wait_ge(setup_pool, 2)
            st.done(dve.tensor_tensor(bias[:], mask_c[:].unsqueeze(1).to_broadcast([P, H_A, 384]),
                                      tab[:, 15, :].unsqueeze(2).to_broadcast([P, H_A, 384]), ALU.add))
            st.done(dve.tensor_scalar(s_sb[:, 0, :], rel[:], float(EDGES[0]), None, ALU.is_ge))
            for h in range(H_A):
                ins = dve.scalar_tensor_tensor(bias[:, h, :], s_sb[:, 0, :], dtab[:, 0, h:h + 1], bias[:, h, :],
                                               ALU.mult, ALU.add)
            st.done(ins)
            dve.sem_inc(tab_ready, 1)

            def lo_tile(dst, chunks, gains, b):
                for kk, c in enumerate(chunks):
                    src, hi = b[:, kk * SEQ:(kk + 1) * SEQ], dst[:, c, 0, :].bitcast(F32)
                    if gains is None:
                        ins = dve.tensor_tensor(dst[:, c, 1, :], src, hi, ALU.subtract)
                    else:
                        ins = dve.scalar_tensor_tensor(dst[:, c, 1, :], src, gains[kk], hi, ALU.mult, ALU.subtract)
                return ins

            for i in range(H1_BEFORE):
                dve.wait_ge(tsplit_hi, i + 1)
                lo_tile(*tsplit_job(("h1", i)), ps[:, 4 + i % 4, :]).then_inc(bank_free[i % 4], 1)
                if i < SPL:
                    split_lo(i, i, i + 1, piece_width(i))
            dve.sem_inc(x_ready, 8)
            for tb in range(TB):
                ins = dve.tensor_scalar(ang[:, tb, :], inv, posq[:, tb:tb + 1], None, ALU.mult)
            st.done(ins)
            inv2pi, magic = float(np.float32(0.5 / np.pi)), 12582912.0
            c1 = 6.28125
            c2 = float(np.float32(np.round((2 * np.pi - c1) * 2 ** 21) / 2 ** 21))
            c3 = float(np.float32(2 * np.pi - c1 - c2))
            for a, quarter in enumerate((0.25, 0.0)):
                t = trig[:, a]
                st.done(dve.tensor_scalar(t, ang[:], inv2pi, quarter, ALU.mult, ALU.add))
                st.done(dve.tensor_scalar(t, t, magic, None, ALU.add))
                st.done(dve.tensor_scalar(t, t, magic, None, ALU.subtract))
                r = kr[:, :, 0:HR]
                st.done(dve.scalar_tensor_tensor(r, t, -c1, ang[:], ALU.mult, ALU.add))
                st.done(dve.scalar_tensor_tensor(r, t, -c2, r, ALU.mult, ALU.add))
                st.done(dve.scalar_tensor_tensor(r, t, -c3, r, ALU.mult, ALU.add))
                st.done(dve.tensor_scalar(r, r, float(quarter * 2 * np.pi), None, ALU.add))
                st.done(dve.tensor_scalar(t, r, 3.1415925, -3.1415925, ALU.min, ALU.max))
            dve.sem_inc(setup_dve, 1)
            SET = st.n

            def rsqrt(out, a, b, parts):
                o = a
                for src, n, w in parts:
                    dve.tensor_scalar(var[:, o:o + w], src, 1.0 / n, EPS, ALU.mult, ALU.add)
                    ins = dve.tensor_scalar(nvar[:, o:o + w], src, -0.5 / n, -0.5 * EPS, ALU.mult, ALU.add)
                    o += w
                assert o == b
                st.done(ins)
                st.done(dve.tensor_scalar(out.bitcast(I32), var[:, a:b].bitcast(I32), -0.5, RSQRT_BITS, ALU.mult, ALU.add))
                t = rtmp[:, a:b]
                for _ in range(3):
                    if b - a == 2:
                        for c in range(2):
                            y = out[:, c:c + 1]
                            ins = dve.tensor_scalar(t[:, c:c + 1], y, y, nvar[:, a + c:a + c + 1], ALU.mult, ALU.mult)
                        st.done(ins)
                    else:
                        st.done(dve.tensor_tensor(t, out, out, ALU.mult))
                        st.done(dve.tensor_tensor(t, t, nvar[:, a:b], ALU.mult))
                    st.done(dve.scalar_tensor_tensor(out, t, 1.5, out, ALU.add, ALU.mult))

            with dve.Fori(0, DEPTH) as l:
                st.base, st.n = l * DVE_STEPS + SET, 0

                def split(p):
                    split_lo(p % SPL, p % RAW, l * NPIECES + p + 1, piece_width(p % NPIECES))

                def split_dyn(p0, j, i, per):
                    q = p0 + j
                    split_lo(q % SPL, q % RAW, l * NPIECES + i * per + (q + 1))

                def read_bank(item):
                    dve.wait_ge(*item_done(l, item))
                    return bank(item)

                def free_bank(ins, item):
                    ins.then_inc(bank_free[ITEM[item] % 4], 1)

                def tsplit(item):
                    dve.wait_ge(tsplit_hi, l * NTSPLIT + (H1_BEFORE + TSPLIT[item] + 1))
                    free_bank(lo_tile(*tsplit_job(item), bank(item)), item)

                def t_evac(g, dst, factors):
                    dve.wait_ge(t_lo_ready, l * len(T_GROUPS) + T_GROUPS.index(g) + 1)
                    st.done(dve.tensor_tensor(dst, ps[:, 2 * (g % 2):2 * (g % 2) + 2, 0:SEQ], t_lo[:], ALU.add))
                    dve.tensor_tensor(dst, dst, factors[:].unsqueeze(1).to_broadcast([P, 2, SEQ]), ALU.mult).then_inc(
                        acc_free[g % 2], 1)

                def y_gain(g, yk, yt, gt):
                    k = yk % 4
                    dve.wait_ge(gain_here, l * 48 + 16 * (yk // 4 + 1))
                    dve.wait_ge(*pieces_used(l, GROUP_END[g]))
                    for tb in (1, 0):
                        if tb == 0:
                            dve.wait_ge(y_sq, l * 24 + 2 * yk + 1)
                        ins = dve.tensor_tensor(yt[:, 2 * k:2 * k + 2, tb, :],
                                                acc(g, tb).rearrange("p (b n) -> p b n", n=256),
                                                gt[:, 512 * k:512 * k + 512].rearrange("p (b n) -> p b n", n=256), ALU.mult)
                        if tb == 1:
                            ins.then_inc(y_half, 1)
                    st.done(ins)
                    dve.wait_ge(y_sq, l * 24 + 2 * yk + 2)
                    dve.sem_inc(acc_free[g % 2], 1)

                def y_rstd():
                    st.done(dve.tensor_reduce(ysum[:], ysq[:], AX, ALU.add))
                    rsqrt(rst[:, 0:TB], 0, TB, [(ysum[:], D, TB)])

                def x_update(yt, i):
                    for tb in range(TB):
                        c = slice(256 * i, 256 * i + 256)
                        ins = dve.scalar_tensor_tensor(x[:, tb, c], yt[:, i, tb, :], rst[:, tb:tb + 1], x[:, tb, c],
                                                       ALU.mult, ALU.add)
                    ins.then_inc(x_ready, 1)

                for step in STEPS:
                    kind = step[0]
                    if kind == "split":
                        split(step[1])
                    elif kind == "evac":
                        gi = step[1]
                        if gi >= G_OUT:
                            if gi < G_MEMK:
                                y_gain(gi, gi - G_OUT, y_a, gain_a)
                            elif gi < G_WQ:
                                if gi == G_MEMK:
                                    dve.wait_ge(*item_read(l, ("R", "mem")))
                                k = gi - G_MEMK
                                t_evac(gi, kx_t[:, 2 * k:2 * k + 2, :], rm_t)
                            elif gi < G_MEMV:
                                if gi == G_WQ:
                                    dve.wait_ge(*item_read(l, ("R", "h2")))
                                k = gi - G_WQ
                                t_evac(gi, qx_t[:, 2 * k:2 * k + 2, :], r_t)
                            elif gi >= G_WO:
                                y_gain(gi, 4 + gi - G_WO, y_a, gain_a)
                            continue
                        name = W_IN_GROUPS[gi][0]
                        if W_IN_GROUPS[gi][1] == "T":
                            if name == "qb0":
                                dve.wait_ge(*item_read(l, ("R", "h1")))
                            if name == "qa0":
                                dve.wait_ge(bias_done, 1)
                            t, i = {"qa": qa_t, "ka": ka_t, "qb": qb_t, "kb": kb_t}[name[:2]], int(name[2])
                            t_evac(gi, t[:, 2 * i:2 * i + 2, :], r_t)
                    elif step == ("latent", "rstd"):
                        dve.wait_ge(lat_sq, l + 1)
                        rsqrt(rst[:, 0:4], 0, 4, [(ssq[:, 0:2], Q_LORA, 2), (ssq[:, 2:4], KV_LORA, 2)])
                        dve.sem_inc(rst_ready, 1)
                    elif step == ("latent", "rope_k"):
                        dve.wait_ge(*acc_read(l, GROUP["ckv"]))
                        dve.wait_ge(setup_act, 1)
                        k1, k2 = ckv[:, :, 256:256 + HR], ckv[:, :, 256 + HR:256 + 2 * HR]
                        ra, rb = rope_b[:, :, 0, :], rope_c[:, :, 0, :]
                        dve.tensor_tensor(kr[:, :, 0:HR], k1, trig[:, 0], ALU.mult)
                        dve.tensor_tensor(ra, k2, trig[:, 1], ALU.mult)
                        dve.tensor_tensor(kr[:, :, HR:], k2, trig[:, 0], ALU.mult)
                        st.done(dve.tensor_tensor(rb, k1, trig[:, 1], ALU.mult))
                        dve.tensor_tensor(kr[:, :, 0:HR], kr[:, :, 0:HR], ra, ALU.subtract)
                        st.done(dve.tensor_tensor(kr[:, :, HR:], kr[:, :, HR:], rb, ALU.add))
                    elif kind in ("latent_T", "head_T", "mem_T", "h1", "h2", "h3", "XO"):
                        tsplit(step)
                    elif kind == "x_rstd":
                        dve.wait_ge(x_sq, l * 6 + 2 * step[1] + 2)
                        st.done(dve.tensor_reduce(xsum[:], xsq[:], AX, ALU.add))
                        rsqrt(rst_x[:], 8, 8 + TB, [(xsum[:], D, TB)])
                        dve.sem_inc(rstx_ready, 1)
                    elif kind == "mem_rstd":
                        dve.wait_ge(mem_sq, l * 2 + 2)
                        rsqrt(rst_m[:], 8, 8 + TB, [(ssq[:, 0:TB], D, TB)])
                        dve.sem_inc(rstm_ready, 1)
                    elif kind == "y_rstd":
                        y_rstd()
                    elif kind == "upd":
                        x_update(y_a, step[2])
                    elif kind == "lam":
                        dve.wait_ge(*item_read(l, ("h1", 7)))
                        dve.tensor_copy(h1_gains[:], h1_gains_all[:, bass.ds(l * KC + KC, KC)])
                        dve.wait_ge(par_here, l * 48 + 48)
                        lp = lam_prod.rearrange("p a h d -> p (a h d)")[:, 0:128].rearrange("p (m d) -> p m d", m=2)
                        lrow = lam_row[:].rearrange("p (m a d) -> p m a d", m=2, a=2)
                        st.done(dve.tensor_tensor(lp, lrow[:, :, 0, :], lrow[:, :, 1, :], ALU.mult))
                        dve.tensor_reduce(lamv[:, 0:2], lp, AX, ALU.add).then_inc(lam_prod_ready, 1)
                        dve.wait_ge(lam_exp_ready, l + 1)
                        st.done(dve.tensor_tensor(lamv[:, 4:5], lamv[:, 3:4], lamv[:, 2:3], ALU.subtract))
                        st.done(dve.tensor_tensor(lamv[:, 4:5], lamv[:, 4:5], rows[:, RINIT:RINIT + 1], ALU.subtract))
                    elif kind == "XS":
                        h = step[1]
                        b = read_bank(step)
                        st.done(dve.tensor_reduce(nmax[:, h, :], b.rearrange("p (t k) -> p t k", t=TB), AX, ALU.max, negate=True))
                        dve.tensor_scalar(nmax[:, h, :], nmax[:, h, :], float(D_X ** -0.5), None, ALU.mult).then_inc(xm_ready, 1)
                    elif kind == "XN":
                        h = step[1]
                        dve.wait_ge(*item_read(l, ("XS", h)))
                        st.done(dve.reciprocal(rcp[:, h, :], sums[:, h, :]))
                        for tb in range(TB):
                            ins = dve.tensor_scalar(px[:, h, tb, :], px[:, h, tb, :], rcp[:, h, tb:tb + 1], None, ALU.mult)
                        ins.then_inc(xpn_ready, 1)
                    elif kind == "rope_q":
                        dve.wait_ge(*acc_read(l, GROUP["uqa"]))
                        dve.wait_ge(*acc_read(l, GROUP["small"]))
                        for tb in range(TB):
                            q1 = q_nat[:, tb, :, D_NOPE:D_NOPE + HR]
                            q2 = q_nat[:, tb, :, D_NOPE + HR:]
                            c = trig[:, 0, tb:tb + 1, :].to_broadcast([P, H_C, HR])
                            s = trig[:, 1, tb:tb + 1, :].to_broadcast([P, H_C, HR])
                            dve.tensor_tensor(rope_a[:, tb], q2, s, ALU.mult)
                            dve.tensor_tensor(rope_b[:, tb], q1, s, ALU.mult)
                            dve.tensor_tensor(rope_c[:, tb], q1, c, ALU.mult)
                            st.done(dve.tensor_tensor(q2, q2, c, ALU.mult))
                            dve.tensor_tensor(q1, rope_c[:, tb], rope_a[:, tb], ALU.subtract)
                            st.done(dve.tensor_tensor(q2, q2, rope_b[:, tb], ALU.add))
                    elif kind == "k_cat":
                        dve.wait_ge(*acc_read(l, GROUP["ukv1"]))
                        for tb in range(TB):
                            ins = dve.tensor_copy(k_cat[:, tb, :, D_NOPE:], kr[:, tb:tb + 1, :].to_broadcast([P, H_C, D_ROPE]))
                        ins.then_inc(k_cat_ready, 1)
                    elif step == ("forget", "abs"):
                        dve.wait_ge(*acc_read(l, GROUP["vbf"]))
                        bf = rows[:, RBF:RBF + 2 * H_B].unsqueeze(1).to_broadcast([P, TB, 2 * H_B])
                        st.done(dve.tensor_tensor(z_f[:], z_f[:], bf, ALU.add))
                        dve.scalar_tensor_tensor(e_f[:], z_f[:], -1.0, z_f[:], ALU.mult, ALU.max).then_inc(f_abs, 1)
                    elif step == ("forget", "one"):
                        dve.wait_ge(f_exp, l + 1)
                        dve.tensor_scalar(e_f[:], e_f[:], 1.0, None, ALU.add).then_inc(f_one, 1)
                        st.done(dve.tensor_scalar(z_f[:], z_f[:], 0.0, None, ALU.min))
                    elif step == ("forget", "log_f"):
                        dve.wait_ge(f_ln, l + 1)
                        dve.tensor_tensor(z_f[:], z_f[:], e_f[:], ALU.subtract).then_inc(lf_ready, 1)
                    elif kind == "forget_scan":
                        n2 = 2 * H_B
                        b = read_bank(step)
                        st.done(dve.memset(lf_ones[0:n2, :], 1.0))
                        ins = dve.tensor_tensor_scan(f_row[0:n2, :], lf_ones[0:n2, :], b[0:n2, 0:SEQ], 0.0, ALU.mult, ALU.add)
                        free_bank(ins, step)
                        dve.wait_ge(*item_read(l, step))
                        st.done(dve.tensor_scalar(f_row[0:n2, :], f_row[0:n2, :], SQ_DB, None, ALU.mult))
                        st.done(dve.tensor_reduce(lamv[0:n2, 6:7], ident[0:n2, 0:H_B], AX, ALU.add))
                        st.done(dve.tensor_scalar(lamv[0:n2, 7:8], lamv[0:n2, 6:7], -1.0, 1.0, ALU.mult, ALU.add))
                        dve.tensor_scalar(fa[0:n2, :], f_row[0:n2, :], lamv[0:n2, 6:7], lamv[0:n2, 7:8], ALU.mult, ALU.add)
                        st.done(dve.tensor_scalar(f_row[0:n2, :], f_row[0:n2, :], -1.0, None, ALU.mult))
                        for h in range(H_B):
                            ins = dve.tensor_scalar(fb[0:n2, h, :], f_row[0:n2, :], ident[0:n2, H_B + h:H_B + h + 1],
                                                    ident[0:n2, h:h + 1], ALU.mult, ALU.add)
                        ins.then_inc(fab_ready, 1)
                    elif kind == "S":
                        n = step[1]
                        hk, h = HEAD_SEQ[n]
                        scale = {"A": DK_A, "B": D_B, "C": DQ_C}[hk] ** -0.5
                        if hk == "A":
                            dve.wait_ge(bias_done, 1)
                        else:
                            dve.wait_ge(setup_pool, 2)
                        tile = bias[:, h, :] if hk == "A" else (mask_b if hk == "B" else mask_c)[:]
                        for job in jobs_of(n):
                            j = JOB[job]
                            b = read_bank(("S", job))
                            if j >= 3:
                                prev = next(m for (m, mm_) in JOB if JOB[(m, mm_)] == j - 3)
                                dve.wait_ge(*item_done(l, ("T", prev)))
                            s = s_sb[:, j % 3, :]
                            ins = dve.scalar_tensor_tensor(s, b[:, 0:384], float(scale), tile, ALU.mult, ALU.add)
                            free_bank(ins, ("S", job))
                            dve.wait_ge(*item_read(l, ("S", job)))
                            dve.tensor_reduce(nmax[:, j % 4, 0:1], s[:, 0:P], AX, ALU.max, negate=True)
                            dve.tensor_reduce(nmax[:, j % 4, 1:2], s[:, P:384], AX, ALU.max, negate=True).then_inc(s_ready, 1)
                    elif kind == "N":
                        n = step[1]
                        hk, h = HEAD_SEQ[n]
                        jl = JOB[jobs_of(n)[-1]]
                        dve.wait_ge(p_ready, l * len(JOB) + jl + 1)
                        if hk == "A":
                            j0 = jl - 1
                            s0, s1 = s_sb[:, j0 % 3, :], s_sb[:, jl % 3, :]
                            dve.reciprocal(o_r[:, :, h], sums[:, j0 % 4, :])
                            st.done(dve.reciprocal(rcp[:, 1, :], sums[:, jl % 4, :]))
                            st.done(dve.scalar_tensor_tensor(rcp[:, 1, :], sums[:, j0 % 4, :], lamv[:, 4:5], rcp[:, 1, :],
                                                             ALU.mult, ALU.mult))
                            for tb, (o, nk) in enumerate(((0, P), (P, SEQ))):
                                ins = dve.scalar_tensor_tensor(s0[:, o:o + nk], s1[:, o:o + nk], rcp[:, 1, tb:tb + 1],
                                                               s0[:, o:o + nk], ALU.mult, ALU.add)
                            ins.then_inc(pn_ready, 1)
                        else:
                            col = (H_A if hk == "B" else H_A + H_B) + h
                            st.done(dve.reciprocal(o_r[:, :, col], sums[:, jl % 4, :]))
                    elif kind == "O":
                        n = step[1]
                        hk, h = HEAD_SEQ[n]
                        col = {"A": 0, "B": H_A, "C": H_A + H_B}[hk] + h
                        b = read_bank(step)
                        ins = dve.tensor_copy(o_nat[:, :, col * P:(col + 1) * P], b[:, 0:2 * P].rearrange("p (t d) -> p t d", t=TB))
                        free_bank(ins, step)
                    elif kind == "onorm":
                        h0 = step[1]
                        h1, n = BATCHES[h0]
                        nh = h1 - h0
                        dve.wait_ge(osq_ready, l * HEADS + n + 1)
                        v, r = o_sq[:, :, h0:h1], o_r[:, :, h0:h1]
                        st.done(dve.tensor_tensor(v, v, r, ALU.mult))
                        flat = ssq[:, 0:TB * nh].rearrange("p (t h) -> p t h", t=TB)
                        st.done(dve.tensor_tensor(flat, v, r, ALU.mult))
                        rsqrt(rst[:, 0:TB * nh], 0, TB * nh, [(ssq[:, 0:TB * nh], P, TB * nh)])
                        st.done(dve.tensor_tensor(v, rst[:, 0:TB * nh].rearrange("p (t h) -> p t h", t=TB), r, ALU.mult))
                        if h0 == 0:
                            st.done(dve.tensor_scalar(v, v, rows[:, RINIT + 1:RINIT + 2], None, ALU.mult))
                        for tb in range(TB):
                            o = o_nat[:, tb, h0 * P:h1 * P].rearrange("p (h d) -> p h d", d=P)
                            ins = dve.tensor_tensor(o, o, v[:, tb].unsqueeze(2).to_broadcast([P, nh, P]), ALU.mult)
                        ins.then_inc(on_ready, 1)

                dve.wait_ge(*item_read(l, ("R", "h3")))
                dve.sem_inc(gate, 1)
                def up_split(i, half, j):
                    split_dyn(P_UP + 8 * half + SPL, j, i, 16)

                def up_tail(i, half, j):
                    g = i * 2 + half
                    if j == 0:
                        dve.wait_ge(up_lo_ready, l * UPG + g + 1)
                        dve.tensor_tensor(up_u[:], ps[:, 4 * half:4 * half + 4, 0:SEQ], up_lo[:], ALU.add).then_inc(up_sum, 1)
                        dve.wait_ge(up_sum, l * UPG + g + 1)
                        dve.tensor_tensor(up_u[:], up_u[:], r_t[:].unsqueeze(1).to_broadcast([P, 4, SEQ]), ALU.mult).then_inc(
                            up_free[half], 1)
                    if j == 2:
                        dve.wait_ge(up_aff_ready, l * UPG + g + 1)
                        for nt in range(4):
                            ins = dve.scalar_tensor_tensor(up_c[:, nt, 1:SEQ], up_u[:, nt, 0:SEQ - 1], cw[:, 4 * nt + 1:4 * nt + 2],
                                                           up_c[:, nt, 1:SEQ], ALU.mult, ALU.add)
                        ins.then_inc(up_tap, 1)
                        dve.wait_ge(up_tap, l * UPG + g + 1)
                        for nt in range(4):
                            ins = dve.scalar_tensor_tensor(up_c[:, nt, 2:SEQ], up_u[:, nt, 0:SEQ - 2], cw[:, 4 * nt:4 * nt + 1],
                                                           up_c[:, nt, 2:SEQ], ALU.mult, ALU.add)
                        ins.then_inc(up_conv_ready, 1)
                    if j == 4:
                        dve.wait_ge(up_gelu_ready, l * UPG + g + 1)
                        dve.tensor_tensor(up_a[:], up_g[:], up_c[:, 2:4, :], ALU.mult).then_inc(up_mul_ready, 1)
                    if j == 6:
                        dve.wait_ge(up_hi_ready, l * UPG + g + 1)
                        dve.tensor_tensor(act_t[:, bass.ds(2 * g, 2), 1, :], up_a[:],
                                          act_t[:, bass.ds(2 * g, 2), 0, :].bitcast(F32), ALU.subtract).then_inc(act_ready, 1)

                with dve.Fori(0, UPG // 2 - 1) as i:
                    for j in range(8):
                        up_split(i, 1, j)
                        up_tail(i, 0, j)
                    for j in range(8):
                        split_dyn(P_UP + 16 + SPL, j, i, 16)
                        up_tail(i, 1, j)
                for j in range(8):
                    up_split(UPG // 2 - 1, 1, j)
                    up_tail(UPG // 2 - 1, 0, j)
                for j in range(8):
                    split(P_DOWN + SPL + j)
                    up_tail(UPG // 2 - 1, 1, j)
                for j in range(8, 16):
                    split(P_DOWN + SPL + j)
                for k in range(1, 4):
                    y_gain(G_DOWN + k - 1, 8 + k - 1, y_f, gain_f)
                    for j in range(16):
                        if (k, j) != (3, 15):
                            split(P_DOWN + 16 * k + SPL + j)
                y_gain(G_DOWN + 3, 11, y_f, gain_f)
                y_rstd()
                for step in END_STEPS:
                    if step[0] == "upd":
                        x_update(y_f, step[2])
                    else:
                        tsplit(step)
                    if step == ("h1", 0):
                        split(NPIECES - 1 + SPL)
                assert st.n == DVE_STEPS, ("DVE_STEPS", st.n)

        @block.gpsimd
        def _(pool):
            pool.memset(ident[:], 0.0)
            pool.memset(mask_b[:], 0.0)
            pool.memset(mask_c[:], 0.0).then_inc(pool_step, 1)
            pool.wait_ge(pool_step, 1)
            pool.affine_select(out=ident[:], in_=ident[:], compare_op=ALU.not_equal, fill=1.0, base=0,
                               pattern=[[-1, P]], channel_multiplier=1).then_inc(setup_pool, 1)
            pool.affine_select(out=mask_b[:, 0:P], in_=mask_b[:, 0:P], compare_op=ALU.is_ge, fill=NEG, base=0,
                               pattern=[[-1, P]], channel_multiplier=1).then_inc(pool_step, 1)
            pool.affine_select(out=mask_b[:, P:384], in_=mask_b[:, P:384], compare_op=ALU.is_ge, fill=NEG, base=P,
                               pattern=[[-1, SEQ]], channel_multiplier=1).then_inc(pool_step, 1)
            pool.memset(mask_c[0:CHUNK, CHUNK:P], NEG).then_inc(pool_step, 1)
            pool.memset(mask_c[0:CHUNK, 384 - CHUNK:384], NEG).then_inc(pool_step, 1)
            pool.wait_ge(pool_step, 5)
            pool.sem_inc(setup_pool, 1)
            pool.wait_ge(tab_ready, 1)
            def over_heads(row):
                return row.unsqueeze(1).to_broadcast([P, H_A, 384])

            def over_columns(col):
                return col.unsqueeze(2).to_broadcast([P, H_A, 384])

            n = 5
            for j in range(1, 30):
                pool.tensor_scalar(ind[:], rel[:], float(EDGES[j]), None, ALU.is_ge).then_inc(pool_step, 1)
                n += 1
                pool.wait_ge(pool_step, n)
                pool.tensor_tensor(btmp[:], over_heads(ind[:]), over_columns(dtab[:, j, :]), ALU.mult).then_inc(pool_step, 1)
                n += 1
                pool.wait_ge(pool_step, n)
                pool.tensor_tensor(bias[:], bias[:], btmp[:], ALU.add).then_inc(pool_step, 1)
                n += 1
            pool.wait_ge(pool_step, n)
            pool.sem_inc(bias_done, 1)

            with pool.Fori(0, DEPTH) as l:
                pool.wait_ge(par_here, l * 48 + 48)
                pool.sem_inc(gate, 1)
                with pool.Fori(0, UPG // 2) as i:
                    for half in range(2):
                        g = i * 2 + half
                        pool.wait_ge(up_mul_ready, l * UPG + g + 1)
                        pool.tensor_copy(cw[:], cols[:, bass.ds(g * 16 + CCONV, 16)]).then_inc(cw_ready, 1)
                        pool.wait_ge(cw_ready, l * UPG + g + 1)
                        pool.wait_ge(up_free[half], l * (UPG // 2) + i + 2)
                        pool.sem_inc(gate, 1)
                        for nt in range(4):
                            ins = pool.tensor_scalar(up_c[:, nt, :], up_u[:, nt, :], cw[:, 4 * nt + 2:4 * nt + 3],
                                                     cw[:, 4 * nt + 3:4 * nt + 4], ALU.mult, ALU.add)
                        ins.then_inc(up_aff_ready, 1)


def _stream(w):
    def piece(rows_cols, chunks):
        n = rows_cols.shape[1]
        a = rows_cols.reshape(chunks, P, n).transpose(1, 0, 2).reshape(P, chunks * n)
        if a.shape[1] < PW:
            a = np.concatenate([a, np.zeros((P, PW - a.shape[1]), a.dtype)], axis=1)
        return a

    out = np.zeros((DEPTH * NPIECES + SPL, P, PW), np.float32)
    n = 0

    def put(mat, chunks):
        nonlocal n
        rows_ = chunks * P
        for k in range(mat.shape[0] // rows_):
            out[n] = piece(mat[k * rows_:(k + 1) * rows_], chunks)
            n += 1

    for l in range(DEPTH):
        w_in, uq, ukv = w["w_in"][l], w["w_uq"][l], w["w_ukv"][l]
        f = w_in[:, C_F:C_F + H_B]
        cols_ = {"cq": w_in[:, C_CQ:C_CQ + Q_LORA], "ckv": w_in[:, C_CKV:C_CKV + KV_LORA + D_ROPE],
                 "va": w_in[:, C_VA:C_VA + 512], "vb": w_in[:, C_VB:C_VB + 512],
                 "vbf": np.concatenate([w_in[:, C_VB + 512:C_VB + 768], f, f], axis=1)}
        for name, kind, _, chunks, _ in W_IN_GROUPS:
            if kind == "T":
                c0 = {"qa": C_QA, "ka": C_KA, "qb": C_QB, "kb": C_KB}[name[:2]] + 256 * int(name[2])
                put(w_in[:, c0:c0 + 256], chunks)
            elif name == "uqa":
                put(uq[:, 0:512], 2)
            elif name == "small":
                put(uq[:, 512:576], 2)
                put(ukv[:, 1024:1152], 1)
            elif name in ("ukv0", "ukv1"):
                put(ukv[:, 512 * int(name[3]):512 * int(name[3]) + 512], 2)
            else:
                put(cols_[name], chunks)
        w_out = w["w_out"][l].reshape(KC, P, D)[HEAD_ORDER].reshape(D, D)
        for k, j in OUT_ORDER:
            put(w_out[256 * j:256 * j + 256, 512 * k:512 * k + 512], 2)
        for k in range(2):
            put(w["wkv_x"][l][:, 256 * k:256 * k + 256], 4)
        for k in range(2):
            put(w["wq_x"][l][:, 256 * k:256 * k + 256], 4)
        put(w["wkv_x"][l][:, 512:1024], 2)
        for k in range(4):
            put(w["wo_x"][l][:, 512 * k:512 * k + 512], 2)
        up = w["w_up"][l].reshape(D, 2, UPG, 256)
        for g in range(UPG):
            put(up[:, :, g].reshape(D, 512), 2)
        for k in range(4):
            put(w["w_down"][l][:, 512 * k:512 * k + 512], 2)
    assert n == DEPTH * NPIECES
    return out


def kernel(**inputs):
    import concourse.bacc as bacc
    from concourse.bass_utils import run_bass_kernel_spmd

    w = {k: np.ascontiguousarray(v) for k, v in inputs.items()}
    cols = np.zeros((DEPTH, P, NCOL), np.float32)
    rows = np.zeros((DEPTH, NROW), np.float32)
    gains = np.zeros((DEPTH * 3, D), np.float32)
    h1_gains = np.zeros((P, (DEPTH + 1) * KC), np.float32)
    for l in range(DEPTH):
        def column(v):
            return v.reshape(-1, P).T
        g = w["norm_gains"][l]
        h1_gains[:, l * KC:(l + 1) * KC] = column(g[0])
        h1_gains[:, (l + 1) * KC:(l + 2) * KC] = column(g[0])
        cols[l, :, CG2:CG2 + KC] = column(g[2])
        cols[l, :, CG4:CG4 + KC] = column(g[4])
        cols[l, :, CMEM:CMEM + KC] = column(w["mem_norm"][l])
        cols[l, :, CHEAD:CHEAD + KC] = column(w["head_norm"][l])
        cols[l, :, CQN:CQN + 4] = column(w["q_norm"][l])
        cols[l, :, CKVN:CKVN + 2] = column(w["kv_norm"][l])
        conv = np.concatenate([w["conv_w"][l], w["conv_b"][l][None]], axis=0)
        conv = conv.reshape(4, 2, UPG, 2, P).transpose(4, 2, 1, 3, 0)
        cols[l, :, CCONV:] = conv.reshape(P, UPG * 16)
        rows[l, RBF:RBF + H_B] = w["b_forget"][l]
        rows[l, RBF + H_B:RBF + 2 * H_B] = w["b_forget"][l]
        init = 0.8 - 0.6 * np.exp(-0.3 * l)
        rows[l, RINIT], rows[l, RINIT + 1] = init, 1.0 - init
        gains[3 * l:3 * l + 3] = g[1::2]
    inv = (10000.0 ** (-np.arange(0, D_ROPE, 2, dtype=np.float64) / D_ROPE)).astype(np.float32)
    arrays = {"stream": _stream(w), "x_in": w["x"].reshape(SEQ, D), "mem_in": w["mem"].reshape(SEQ, D),
              "pos_in": w["positions"].reshape(SEQ), "posq_in": w["positions"].reshape(TB, P).T,
              "first_row_in": np.concatenate([inv, w["rel_bias"].reshape(-1)]), "cols_in": cols,
              "h1_gains_in": h1_gains, "rows_in": rows, "lam_in": w["lam"].reshape(DEPTH, -1), "gains_in": gains}
    arrays = {k: np.ascontiguousarray(a) for k, a in arrays.items()}
    nc = bacc.Bacc("TRN2", target_bir_lowering=False, num_devices=1)
    args = [nc.dram_tensor(n, a.shape, mybir.dt.from_np(a.dtype), kind="ExternalInput").ap() for n, a in arrays.items()]
    out = nc.dram_tensor("out", (SEQ, D), F32, kind="ExternalOutput").ap()
    build(nc, *args, out)
    r = run_bass_kernel_spmd(nc, [arrays], core_ids=[0])
    return r.results[0]["out"].reshape(1, SEQ, D)
```
